# Optimizing a Trainium2 kernel written in Bass

```python
import math
import jax, jax.numpy as jnp
from jax import lax
import numpy as np

D_MODEL = 1024
BATCH = 1
SEQ = 256
DEPTH = 1

N_META = 16
SSD_EXPAND = 2
D_INNER = SSD_EXPAND * D_MODEL
SSD_HEADDIM = 64
SSD_HEADS = D_INNER // SSD_HEADDIM
SSD_GROUPS = 4
SSD_HPG = SSD_HEADS // SSD_GROUPS
D_STATE = 128
CONV_K = 4
CONV_DIM = D_INNER + 2 * SSD_GROUPS * D_STATE
CHUNK = 256
DT_MIN = 1e-3
DT_MAX = 1e-1
MLA_HEADS = 16
QK_NOPE = 64
QK_ROPE = 32
V_HEAD = 64
Q_LORA = 384
KV_LORA = 256
ROPE_THETA = 10000.0
Q_BLOCK = 128
N_EXPERTS = 32
TOP_K = 4
D_EXPERT = D_MODEL
SWIGLU_ALPHA = 1.702
SWIGLU_LIMIT = 7.0
MOE_BLOCK = 256
EPS = 1e-5
MLA_EPS = 1e-6

IN_SPLITS = [
    D_INNER,
    D_INNER + CONV_DIM,
    D_INNER + CONV_DIM + SSD_HEADS,
    D_INNER + CONV_DIM + SSD_HEADS + Q_LORA,
    D_INNER + CONV_DIM + SSD_HEADS + Q_LORA + KV_LORA + QK_ROPE,
]
IN_COLS = IN_SPLITS[-1] + 2 * D_MODEL

kernel_name = "meta_ssd_mla_gated_moe_block"

def rms_norm(x, g, eps=EPS):
    xf = x.astype(jnp.float32)
    y = xf * lax.rsqrt(jnp.mean(xf * xf, axis=-1, keepdims=True) + eps)
    return (y * g.astype(jnp.float32)).astype(x.dtype)

def rope_tables(n_pos, dim):
    pos = jnp.arange(n_pos, dtype=jnp.float32)
    inv = ROPE_THETA ** (-jnp.arange(0, dim, 2, dtype=jnp.float32) / dim)
    ang = pos[:, None] * inv[None, :]
    return jnp.cos(ang), jnp.sin(ang)

def apply_rope(x, cos, sin):
    x1, x2 = jnp.split(x.astype(jnp.float32), 2, axis=-1)
    return jnp.concatenate([x1 * cos - x2 * sin, x2 * cos + x1 * sin], axis=-1).astype(x.dtype)

def causal_depthwise_conv(x, w, b):
    y = lax.conv_general_dilated(
        x, w[:, None, :].astype(x.dtype), window_strides=(1,), padding=[(CONV_K - 1, 0)],
        dimension_numbers=("NWC", "WIO", "NWC"), feature_group_count=x.shape[-1])
    return y + b.astype(x.dtype)

def ssd_scan(xh, dt, a, bm, cm):
    bsz, t = xh.shape[:2]
    nc = t // CHUNK
    xc = xh.reshape(bsz, nc, CHUNK, SSD_GROUPS, SSD_HPG, SSD_HEADDIM)
    dtc = dt.reshape(bsz, nc, CHUNK, SSD_GROUPS, SSD_HPG)
    bc = bm.reshape(bsz, nc, CHUNK, SSD_GROUPS, D_STATE)
    cc = cm.reshape(bsz, nc, CHUNK, SSD_GROUPS, D_STATE)
    a_cs = jnp.cumsum(jnp.moveaxis(dtc * a, 2, -1), axis=-1)
    xdt = xc * dtc[..., None]
    causal = jnp.tril(jnp.ones((CHUNK, CHUNK), dtype=bool))
    decay = jnp.exp(jnp.where(causal, a_cs[..., :, None] - a_cs[..., None, :], -jnp.inf))
    cb = jnp.einsum("bclgn,bcsgn->bcgls", cc, bc)
    scores = cb[:, :, :, None] * decay
    y_diag = jnp.einsum("bcgrls,bcsgrp->bclgrp", scores, xdt)
    decay_states = jnp.moveaxis(jnp.exp(a_cs[..., -1:] - a_cs), -1, 2)
    states = jnp.einsum("bclgn,bclgrp->bcgrpn", bc, xdt * decay_states[..., None])
    chunk_decay = jnp.exp(a_cs[..., -1])

    def step(s, inp):
        st, dec = inp
        return dec[..., None, None] * s + st, s

    s0 = jnp.zeros_like(states[:, 0])
    _, prev = lax.scan(step, s0, (jnp.moveaxis(states, 1, 0), jnp.moveaxis(chunk_decay, 1, 0)))
    prev = jnp.moveaxis(prev, 0, 1)
    state_decay = jnp.moveaxis(jnp.exp(a_cs), -1, 2)
    y_off = jnp.einsum("bclgn,bcgrpn->bclgrp", cc, prev) * state_decay[..., None]
    return (y_diag + y_off).reshape(bsz, t, SSD_GROUPS, SSD_HPG, SSD_HEADDIM)

def ssd_branch(z, xbc, dt_raw, conv_w, conv_b, dt_bias, a_log, d_skip, norm_w):
    bsz, l = z.shape[:2]
    xbc = jax.nn.silu(causal_depthwise_conv(xbc, conv_w, conv_b))
    xs, bm, cm = jnp.split(xbc, [D_INNER, D_INNER + SSD_GROUPS * D_STATE], axis=-1)
    dt = jax.nn.softplus(dt_raw.astype(jnp.float32) + dt_bias.astype(jnp.float32))
    a = -jnp.exp(a_log.astype(jnp.float32)).reshape(SSD_GROUPS, SSD_HPG)
    t_real = l - N_META
    n_real_chunks = -(-t_real // CHUNK)
    front = CHUNK - N_META
    pad = ((0, 0), (front, n_real_chunks * CHUNK - t_real), (0, 0))
    xh = jnp.pad(xs, pad).reshape(bsz, -1, SSD_GROUPS, SSD_HPG, SSD_HEADDIM)
    bp = jnp.pad(bm, pad).reshape(bsz, -1, SSD_GROUPS, D_STATE)
    cp = jnp.pad(cm, pad).reshape(bsz, -1, SSD_GROUPS, D_STATE)
    dtp = jnp.pad(dt, pad).reshape(bsz, -1, SSD_GROUPS, SSD_HPG)
    y = ssd_scan(xh, dtp, a, bp, cp)[:, front:front + l]
    y = y + d_skip.astype(jnp.float32).reshape(SSD_GROUPS, SSD_HPG)[:, :, None] * \
        xs.reshape(bsz, l, SSD_GROUPS, SSD_HPG, SSD_HEADDIM)
    yg = (y.reshape(bsz, l, D_INNER) * jax.nn.silu(z.astype(jnp.float32))).astype(jnp.float32)
    yg = yg.reshape(bsz, l, SSD_GROUPS, D_INNER // SSD_GROUPS)
    yg = yg * lax.rsqrt(jnp.mean(yg * yg, axis=-1, keepdims=True) + EPS)
    return (yg.reshape(bsz, l, D_INNER) * norm_w.astype(jnp.float32)).astype(z.dtype)

def mla_branch(q_a, kv_a, q_norm, w_uq, kv_norm, w_ukv, cos, sin):
    bsz, l = q_a.shape[:2]
    scale = (QK_NOPE + QK_ROPE) ** -0.5
    q = (rms_norm(q_a, q_norm, MLA_EPS) @ w_uq).reshape(bsz, l, MLA_HEADS, QK_NOPE + QK_ROPE)
    q_nope, q_pe = jnp.split(q, [QK_NOPE], axis=-1)
    q_pe = apply_rope(q_pe, cos[:, None], sin[:, None])
    c_kv, k_pe = jnp.split(kv_a, [KV_LORA], axis=-1)
    k_pe = apply_rope(k_pe, cos, sin)
    kv = (rms_norm(c_kv, kv_norm, MLA_EPS) @ w_ukv).reshape(bsz, l, MLA_HEADS, QK_NOPE + V_HEAD)
    k_nope, v = jnp.split(kv, [QK_NOPE], axis=-1)
    n_blocks = -(-l // Q_BLOCK)
    lp = n_blocks * Q_BLOCK
    qpad = ((0, 0), (0, lp - l), (0, 0), (0, 0))
    qn_b = jnp.moveaxis(jnp.pad(q_nope * scale, qpad).reshape(bsz, n_blocks, Q_BLOCK, MLA_HEADS, QK_NOPE), 1, 0)
    qp_b = jnp.moveaxis(jnp.pad(q_pe * scale, qpad).reshape(bsz, n_blocks, Q_BLOCK, MLA_HEADS, QK_ROPE), 1, 0)
    k_idx = jnp.arange(l)

    def attend(blk):
        qn, qp, start = blk
        s = jnp.einsum("bqhd,bkhd->bhqk", qn, k_nope) + jnp.einsum("bqhr,bkr->bhqk", qp, k_pe)
        q_idx = start + jnp.arange(Q_BLOCK)
        s = jnp.where(k_idx[None, :] <= q_idx[:, None], s.astype(jnp.float32), -jnp.inf)
        p = jax.nn.softmax(s, axis=-1).astype(v.dtype)
        return jnp.einsum("bhqk,bkhd->bqhd", p, v)

    starts = jnp.arange(n_blocks, dtype=jnp.int32) * Q_BLOCK
    o = lax.map(attend, (qn_b, qp_b, starts))
    return jnp.moveaxis(o, 0, 1).reshape(bsz, lp, MLA_HEADS * V_HEAD)[:, :l]

def clamped_swiglu(h):
    h_glu, h_lin = h[..., ::2], h[..., 1::2]
    h_glu = jnp.minimum(h_glu, SWIGLU_LIMIT)
    h_lin = jnp.clip(h_lin, -SWIGLU_LIMIT, SWIGLU_LIMIT)
    return h_glu * jax.nn.sigmoid(SWIGLU_ALPHA * h_glu) * (h_lin + 1)

def moe_ffn(xn, w_router, b_router, w1, b1, w2, b2):
    bsz, l, d = xn.shape
    tok_x = xn.reshape(-1, d)
    n_tok = tok_x.shape[0]
    logits = (tok_x @ w_router + b_router).astype(jnp.float32)
    top_logit, top_e = lax.top_k(logits, TOP_K)
    top_w = jax.nn.softmax(top_logit, axis=-1)
    n_assign = n_tok * TOP_K
    flat_e = top_e.reshape(-1)
    order = jnp.argsort(flat_e)
    e_sorted = flat_e[order]
    tok_sorted = (order // TOP_K).astype(jnp.int32)
    w_sorted = top_w.reshape(-1)[order]
    group_sizes = jnp.bincount(flat_e, length=N_EXPERTS).astype(jnp.int32)
    padded_sizes = ((group_sizes + MOE_BLOCK - 1) // MOE_BLOCK) * MOE_BLOCK
    padded_ends = jnp.cumsum(padded_sizes)
    padded_starts = padded_ends - padded_sizes
    group_starts = jnp.cumsum(group_sizes) - group_sizes
    dest = padded_starts[e_sorted] + jnp.arange(n_assign, dtype=jnp.int32) - group_starts[e_sorted]
    n_blocks = -(-n_assign // MOE_BLOCK) + N_EXPERTS
    n_rows = n_blocks * MOE_BLOCK
    row_tok = jnp.full((n_rows,), n_tok, jnp.int32).at[dest].set(tok_sorted)
    row_w = jnp.zeros((n_rows,), jnp.float32).at[dest].set(w_sorted)
    block_e = jnp.minimum(jnp.searchsorted(padded_ends, jnp.arange(n_blocks) * MOE_BLOCK, side="right"),
                          N_EXPERTS - 1).astype(jnp.int32)
    x_pad = jnp.concatenate([tok_x, jnp.zeros((1, d), tok_x.dtype)], axis=0)

    def expert_block(blk):
        tok_blk, w_blk, e = blk
        hb = x_pad[tok_blk] @ w1[e] + b1[e]
        ob = clamped_swiglu(hb) @ w2[e] + b2[e]
        return ob * w_blk[:, None].astype(ob.dtype)

    rows = lax.map(expert_block, (row_tok.reshape(n_blocks, MOE_BLOCK), row_w.reshape(n_blocks, MOE_BLOCK), block_e))
    y = jax.ops.segment_sum(rows.reshape(n_rows, d), row_tok, num_segments=n_tok + 1)[:n_tok]
    return y.reshape(bsz, l, d)

def setup_inputs(seed: int = 0) -> dict:
    key = jax.random.key(seed)
    ks = jax.random.split(key, 32)
    f32 = jnp.float32

    def nrm(k, shape, scale):
        return jax.random.normal(k, shape, f32) * scale

    def gain(k, shape):
        return 1.0 + 0.02 * jax.random.normal(k, shape, f32)

    dt0 = jnp.exp(jax.random.uniform(ks[6], (DEPTH, SSD_HEADS), f32, math.log(DT_MIN), math.log(DT_MAX)))
    return {
        "x": nrm(ks[0], (BATCH, SEQ, D_MODEL), 1.0),
        "meta_tokens": nrm(ks[1], (N_META, D_MODEL), 1.0),
        "norm_mix": gain(ks[2], (DEPTH, D_MODEL)),
        "w_in": nrm(ks[3], (DEPTH, D_MODEL, IN_COLS), D_MODEL ** -0.5),
        "conv_w": nrm(ks[4], (DEPTH, CONV_K, CONV_DIM), CONV_K ** -0.5),
        "conv_b": nrm(ks[5], (DEPTH, CONV_DIM), 0.02),
        "dt_bias": dt0 + jnp.log(-jnp.expm1(-dt0)),
        "a_log": jnp.log(jax.random.uniform(ks[7], (DEPTH, SSD_HEADS), f32, 1.0, 16.0)),
        "d_skip": gain(ks[8], (DEPTH, SSD_HEADS)),
        "ssd_norm": gain(ks[9], (DEPTH, D_INNER)),
        "w_ssd_out": nrm(ks[10], (DEPTH, D_INNER, D_MODEL), D_INNER ** -0.5),
        "q_norm": gain(ks[11], (DEPTH, Q_LORA)),
        "w_uq": nrm(ks[12], (DEPTH, Q_LORA, MLA_HEADS * (QK_NOPE + QK_ROPE)), Q_LORA ** -0.5),
        "kv_norm": gain(ks[13], (DEPTH, KV_LORA)),
        "w_ukv": nrm(ks[14], (DEPTH, KV_LORA, MLA_HEADS * (QK_NOPE + V_HEAD)), KV_LORA ** -0.5),
        "w_o": nrm(ks[15], (DEPTH, MLA_HEADS * V_HEAD, D_MODEL), (MLA_HEADS * V_HEAD) ** -0.5),
        "w_out": nrm(ks[16], (DEPTH, D_MODEL, D_MODEL), D_MODEL ** -0.5),
        "norm_ffn": gain(ks[17], (DEPTH, D_MODEL)),
        "w_router": nrm(ks[18], (DEPTH, D_MODEL, N_EXPERTS), D_MODEL ** -0.5),
        "b_router": nrm(ks[19], (DEPTH, N_EXPERTS), 0.01),
        "w_mlp1": nrm(ks[20], (DEPTH, N_EXPERTS, D_MODEL, 2 * D_EXPERT), D_MODEL ** -0.5),
        "b_mlp1": nrm(ks[21], (DEPTH, N_EXPERTS, 2 * D_EXPERT), 0.02),
        "w_mlp2": nrm(ks[22], (DEPTH, N_EXPERTS, D_EXPERT, D_MODEL), D_EXPERT ** -0.5),
        "b_mlp2": nrm(ks[23], (DEPTH, N_EXPERTS, D_MODEL), 0.02),
        "norm_final": gain(ks[24], (D_MODEL,)),
    }

def reference(x, meta_tokens, norm_mix, w_in, conv_w, conv_b, dt_bias, a_log, d_skip, ssd_norm, w_ssd_out,
              q_norm, w_uq, kv_norm, w_ukv, w_o, w_out, norm_ffn, w_router, b_router,
              w_mlp1, b_mlp1, w_mlp2, b_mlp2, norm_final):
    bsz = x.shape[0]
    meta = jnp.broadcast_to(meta_tokens[None].astype(x.dtype), (bsz, N_META, D_MODEL))
    h = jnp.concatenate([meta, x], axis=1)
    l = h.shape[1]
    cos, sin = rope_tables(l, QK_ROPE)
    for i in range(DEPTH):
        hn = rms_norm(h, norm_mix[i])
        u = hn @ w_in[i]
        z, xbc, dt_raw, q_a, kv_a, gate_logits = jnp.split(u, IN_SPLITS, axis=-1)
        y_ssd = ssd_branch(z, xbc, dt_raw, conv_w[i], conv_b[i], dt_bias[i], a_log[i], d_skip[i],
                           ssd_norm[i]) @ w_ssd_out[i]
        y_mla = mla_branch(q_a, kv_a, q_norm[i], w_uq[i], kv_norm[i], w_ukv[i], cos, sin) @ w_o[i]
        g_ssd, g_mla = jnp.split(jax.nn.sigmoid(gate_logits), 2, axis=-1)
        h = h + (g_ssd * y_ssd + g_mla * y_mla).astype(h.dtype) @ w_out[i]
        h = h + moe_ffn(rms_norm(h, norm_ffn[i]), w_router[i], b_router[i], w_mlp1[i], b_mlp1[i],
                        w_mlp2[i], b_mlp2[i]).astype(h.dtype)
    return rms_norm(h, norm_final)[:, N_META:]


_drawn_inputs = setup_inputs


def setup_inputs(seed=0):
    import zlib

    import numpy as np

    out = dict(_drawn_inputs(seed))
    spreads = {}
    factors = {'q_norm': 3.703,
     'kv_norm': 3.637,
     'b_mlp1': 5.654,
     'b_mlp2': 17.331,
     'norm_final': 23.255,
     'conv_b': 4.164,
     'd_skip': 20.157,
     'ssd_norm': 13.436,
     'b_router': 9.619,
     'norm_ffn': 4.107}
    for name, (base, spread) in spreads.items():
        noise = np.random.default_rng([zlib.crc32(name.encode()), seed]).standard_normal(out[name].shape)
        drawn = base * np.exp(spread * noise) if base else spread * noise
        out[name] = __import__('jax').numpy.asarray(drawn.astype(out[name].dtype))
    for name, factor in factors.items():
        out[name] = (out[name] * factor).astype(out[name].dtype)
    return out
```

```python
import concourse.bass as bass
from concourse import mybir
from contextlib import ExitStack

F32 = mybir.dt.float32
I32 = mybir.dt.int32
U32 = mybir.dt.uint32
ALU = mybir.AluOpType
ACT = mybir.ActivationFunctionType
AX = mybir.AxisListType

P = 128
D = 1024
KD = D // P
NMETA, SEQ = 16, 256
NB = 3
T = NB * P
T0 = P - NMETA
L = NMETA + SEQ
DI = 2048
NX = DI // P
HEADS_S = 32
GROUPS = 4
CHUNKS_PER_GROUP = NX // GROUPS
MH = 16
NOPE, ROPE, VH = 64, 32, 64
QH = NOPE + ROPE
QL, KVL = 384, 256
KQ, KKV = QL // P, KVL // P
E = 32
TOPK = 4
DE = 1024
SLOTS = 64
EPS, MLA_EPS = 1e-5, 1e-6
ALPHA, LIMIT = 1.702, 7.0
NEG = -1.0e30

Z0, XS0, B0, C0 = 0, DI, 2 * DI, 2 * DI + GROUPS * P
DT0 = C0 + GROUPS * P
QA0 = DT0 + HEADS_S
KV0 = QA0 + QL
G0 = KV0 + KVL + ROPE
DKV = HEADS_S + KVL + ROPE

SLABS = [("dkv", KD * DKV), ("qa", KD * QL), ("B", KD * 512), ("C", KD * 512),
         ("uq0", KQ * 768), ("uq1", KQ * 768), ("ukv", KKV * 2048)]
SLABS += [(f"xs{i}", KD * 512) for i in range(4)] + [(f"z{i}", KD * 512) for i in range(4)]
SLABS += [(f"g{i}", KD * 512) for i in range(4)] + [(f"wo{i}", KD * 512) for i in range(2)]
SLABS += [(f"so{i}", NX * 256) for i in range(4)] + [(f"wout{i}", KD * 512) for i in range(2)]
SLAB = {name: i for i, (name, _) in enumerate(SLABS)}
OFF = [sum(n for _, n in SLABS[:i]) for i in range(len(SLABS))]
SLAB_COLS = OFF[-1] + SLABS[-1][1]
NSLOT, SLOT = 6, 4096

W1_AT = [(3, 0), (3, 2048), (4, 0), (4, 2048), (5, 0), (5, 2048), (0, 0), (0, 2048)]
W2_AT = [(1, 0), (1, 2048), (2, 0), (2, 2048)]
CHUNKS = len(W1_AT) + len(W2_AT)

VEC = {}
_at = 0
for _name, _n in [("norm_mix", KD), ("conv_w", 4 * 24), ("conv_b", 24), ("ssd_norm", NX), ("d_skip", NX),
                  ("q_norm", KQ), ("kv_norm", KKV), ("dt_bias", E), ("a_log", E), ("b_router", E),
                  ("cos", NB * 16), ("sin", NB * 16), ("w_router", KD * E)]:
    VEC[_name] = (_at, _at + _n)
    _at += _n
VEC_COLS = _at


def meta_ssd_mla_moe(nc, x, meta, slabs, vecs, rows, w1, b1, w2, b2, out):
    ctx = ExitStack()
    with ctx:
        def sb(name, cols, dt=F32):
            return ctx.enter_context(nc.sbuf_tensor(name, [P, cols], dt))

        ring = sb("ring", NSLOT * SLOT)
        work = sb("work", 25736)
        vec = sb("vec", VEC_COLS)
        ident = sb("ident", P)
        ones = sb("ones", P)
        metarows = sb("metarows", 2 * P)
        tri = sb("tri", 2 * P)
        trimeta = sb("trimeta", P)
        keymask = sb("keymask", L)
        iota_slot = sb("iota_slot", SLOTS)
        iota_e = sb("iota_e", E)
        small = sb("small", 804)
        idx = sb("idx", 16, U32)
        cmax_i = sb("cmax_i", 1, I32)
        bank = [ctx.enter_context(nc.psum_tensor(f"bank{i}", [P, 512], F32)) for i in range(8)]

        def w(at, n):
            return work[:, at:at + n]

        def sm(at, n):
            return small[:, at:at + n]

        def v(name, i=0, n=None):
            a, b = VEC[name]
            return vec[:, a + i:(b if n is None else a + i + n)]

        hnT = w(0, 3072).rearrange("p (k t) -> p k t", k=KD)
        xT = w(3072, 6144).rearrange("p (c t) -> p c t", c=NX)
        BT = w(9216, 1536).rearrange("p (g t) -> p g t", g=GROUPS)
        CT = w(10752, 1024).rearrange("p (g t) -> p g t", g=GROUPS)
        attnT = w(11776, 2048).rearrange("p (k t) -> p k t", k=KD)
        R = 13824
        xtok = w(R, 3072).rearrange("p (b d) -> p b d", b=NB)
        q_sb = w(R, 3072).rearrange("p (b d) -> p b d", b=2)
        V = w(R + 3072, 3072).rearrange("p (b d) -> p b d", b=NB)
        mid = w(R + 3072, 960).rearrange("p (b d) -> p b d", b=NB)
        qa = w(R + 4032, 768).rearrange("p (b d) -> p b d", b=2)
        ckk = w(R + 4800, 1056).rearrange("p (b d) -> p b d", b=NB)
        ckvT = w(R + 6144, 768).rearrange("p (k t) -> p k t", k=KKV)
        qaT = w(R + 6912, 768).rearrange("p (k t) -> p k t", k=KQ)
        pT = w(R + 6912, 640)
        kTh = w(R + 7680, 544).rearrange("p (i t) -> p i t", i=2)
        qTh = w(R + 8224, 512).rearrange("p (i t) -> p i t", i=2)
        probs = w(R + 8736, 1536).rearrange("p (i b t) -> p i b t", i=2, b=2)
        xraw = w(R + 10272, 550).rearrange("p (i t) -> p i t", i=2)
        conv = w(R + 10822, 544).rearrange("p (i t) -> p i t", i=2)
        convt = w(R + 11366, 544).rearrange("p (i t) -> p i t", i=2)
        junk = w(3072, 3072).rearrange("p (b d) -> p b d", b=NB)
        junk2 = w(6144, 2048)
        ropet = w(3072, 2048).rearrange("p (i h r) -> p i h r", i=8, r=16)
        y2T = w(R, 4096).rearrange("p (c t) -> p c t", c=NX)
        CBm = w(R + 4096, 2560).rearrange("p (g t) -> p g t", g=GROUPS)
        decay = w(R + 6656, 2560).rearrange("p (i j t) -> p i j t", i=2, j=2)
        xdt = w(R + 9216, 768).rearrange("p (i b t) -> p i b t", i=2, b=NB)
        ztanh = w(R + 9984, 512).rearrange("p (i t) -> p i t", i=2)
        zcopy = w(R + 10496, 512).rearrange("p (i t) -> p i t", i=2)
        ysq = w(R + 11008, 512).rearrange("p (i t) -> p i t", i=2)
        zw = w(9216, 256)
        yv = w(9472, 256)
        var_g = w(9728, GROUPS * 256)
        rstd_g, tmp_g = w(R + 6656, GROUPS * 256), w(R + 7680, GROUPS * 256)
        gt = w(3072, 4096).rearrange("p (c t) -> p c t", c=16)
        mT = w(7168, 2048).rearrange("p (k t) -> p k t", k=KD)
        mtmp = w(9984, 512).rearrange("p (i t) -> p i t", i=2)
        xres = w(R + 4096, 2048).rearrange("p (b d) -> p b d", b=2)
        h1 = w(R, 2048).rearrange("p (b d) -> p b d", b=2)
        xn = w(R + 2048, 2048).rearrange("p (b d) -> p b d", b=2)
        xnT = w(R + 6656, 2048).rearrange("p (b k t) -> p b k t", b=2, k=KD)
        hsq = w(R + 8704, 2048).rearrange("p (i d) -> p i d", i=4)
        chosen = w(9216, 256).rearrange("p (b j e) -> p b j e", b=2, j=TOPK)
        nf = w(11776, 1024)
        nfin = w(12800, 1024)
        b1all = w(0, 2048)
        b2all = w(2048, 1024)
        xg = w(3072, 512)
        xgT = w(3584, 512).rearrange("p (j t) -> p j t", j=4)
        actT = w(4096, 512).rearrange("p (j t) -> p j t", j=4)
        glu = w(4608, 512)
        lin = w(5120, 512)
        sig = w(5632, 512)
        act = w(6144, 512)
        ob = w(6656, 512)
        scat = w(7168, 512).rearrange("p (n t) -> p n t", n=2)
        hot = w(7680, 128).rearrange("p (b s) -> p b s", b=2)
        hotw = w(7808, 256).rearrange("p (b i s) -> p b i s", b=2, i=2)
        bsel = w(8064, SLOTS)
        pw = w(8128, 4)
        wpad = w(5632, 256).rearrange("p (b t) -> p b t", b=2)
        fin = w(4096, 2048).rearrange("p (b d) -> p b d", b=2)

        ssx, ssk, ssq = sm(0, 3), sm(3, 3), sm(6, 2)
        rsx, rsk, rsq = sm(8, 3), sm(11, 3), sm(14, 2)
        dtv, dta, dt = sm(16, 96), sm(112, 96), sm(208, 96)
        dA, As = sm(304, 96), sm(400, 96)
        AT = sm(496, 256)
        negA = sm(752, 32)
        rmax, nmax = sm(784, 2), sm(786, 4).rearrange("p (i b) -> p i b", i=2)
        rsum = sm(790, 4).rearrange("p (i b) -> p i b", i=2)
        rinv = sm(794, 2)
        kr = w(R + 6912, 192).rearrange("p (i b r) -> p i b r", i=4, b=NB)
        wTs = sm(208, 256)
        lg = sm(16, 64).rearrange("p (b e) -> p b e", b=2)
        mx8 = sm(80, 16).rearrange("p (b e) -> p b e", b=2)
        idxf = sm(96, 16).rearrange("p (b e) -> p b e", b=2)
        e4 = sm(112, 8).rearrange("p (b e) -> p b e", b=2)
        nm4, s4, r4 = sm(120, 2), sm(122, 2), sm(124, 2)
        mask = sm(496, 64).rearrange("p (b e) -> p b e", b=2)
        rsn = sm(564, 2)
        ssh4 = sm(560, 4).rearrange("p (b n) -> p b n", b=2)
        PW = sm(624, 132).rearrange("p (i e) -> p i e", i=4)
        ssh, rsh, cmax = sm(796, 2), sm(798, 2), sm(800, 1)
        nrt = sm(801, 3)

        def sem(name):
            return ctx.enter_context(nc.semaphore(name))

        vec_in, x_in = sem("vec_in"), [sem(f"x_in{b}") for b in range(NB)]
        slab_in = [sem(f"slab_in{i}") for i in range(NSLOT)]
        xres_in, rows_in, bias_in = sem("xres_in"), sem("rows_in"), sem("bias_in")
        w1_in = [sem(f"w1_in{i}") for i in range(len(W1_AT))]
        w2_in = [sem(f"w2_in{i}") for i in range(len(W2_AT))]
        chunk_used = sem("chunk_used")
        pool_step, dve_step, act_step = sem("pool_step"), sem("dve_step"), sem("act_step")
        consts_ready, zeros_ready, meta_zero = sem("consts_ready"), sem("zeros_ready"), sem("meta_zero")
        x_squared, hn_ready, hn_trans, hnT_ready = sem("x_squared"), sem("hn_ready"), sem("hn_trans"), sem("hnT_ready")
        proj_done, proj_read = sem("proj_done"), sem("proj_read")
        latent_ready, latent_trans, latentT_ready = sem("latent_ready"), sem("latent_trans"), sem("latentT_ready")
        kpeT_ready, dt_abs, dt_ln, dA_ready = sem("kpeT_ready"), sem("dt_abs"), sem("dt_ln"), sem("dA_ready")
        cum_done, cum_read = sem("cum_done"), sem("cum_read")
        conv_done, conv_tanh, conv_fin = sem("conv_done"), sem("conv_tanh"), sem("conv_fin")
        q_roped = sem("q_roped")
        qk_done, kT_ready, qT_ready = sem("qk_done"), sem("kT_ready"), sem("qT_ready")
        scores_done, scores_read, exp_done, probs_ready = sem("scores_done"), sem("scores_read"), sem("exp_done"), sem("probs_ready")
        pT_done, pTa_ready, pTb_ready = sem("pT_done"), sem("pTa_ready"), sem("pTb_ready")
        pv_done, pv_read = sem("pv_done"), sem("pv_read")
        cb_done, cb_read = sem("cb_done"), sem("cb_read")
        acum_done, diff_ready, decay_exp, sc_ready = sem("acum_done"), sem("diff_ready"), sem("decay_exp"), sem("sc_ready")
        xtr_done, xdt_ready = sem("xtr_done"), sem("xdt_ready")
        ssdy_done, ssdy_read, y2_ready, ysq_ready = sem("ssdy_done"), sem("ssdy_read"), sem("y2_ready"), sem("ysq_ready")
        gsum_done, gsum_read, yn_ready = sem("gsum_done"), sem("gsum_read"), sem("yn_ready")
        out_done, merged = sem("out_done"), sem("merged")
        wout_done, h1_ready, h1_squared, xn_ready = sem("wout_done"), sem("h1_ready"), sem("h1_squared"), sem("xn_ready")
        xn_trans, xnT_ready, xn_scaled = sem("xn_trans"), sem("xnT_ready"), sem("xn_scaled")
        rsn_ready, mask_ready, w_trans = sem("rsn_ready"), sem("mask_ready"), sem("w_trans")
        logits_done, top_ready, top_exp, route_ready = sem("logits_done"), sem("top_ready"), sem("top_exp"), sem("route_ready")
        pos_done, wT_ready, count_ready = sem("pos_done"), sem("wT_ready"), sem("count_ready")
        moe_zero, moe_step = sem("moe_zero"), sem("moe_step")
        hot_ready, hotw_ready, bsel_ready = sem("hot_ready"), sem("hotw_ready"), sem("bsel_ready")
        gather_done, xg_ready, xg_trans, xgT_ready = sem("gather_done"), sem("xg_ready"), sem("xg_trans"), sem("xgT_ready")
        up_done, glu_ready, up_read, sig_ready = sem("up_done"), sem("glu_ready"), sem("up_read"), sem("sig_ready")
        act_ready, scat_trans, scat_ready, act_trans, actT_ready = (sem("act_ready"), sem("scat_trans"), sem("scat_ready"),
                                                                   sem("act_trans"), sem("actT_ready"))
        down_done, ob_ready, scattered = sem("down_done"), sem("ob_ready"), sem("scattered")
        h2_ready, h2_squared, y_ready, y_out = sem("h2_ready"), sem("h2_squared"), sem("y_ready"), sem("y_out")

        ORDER = (1, 2, 0)
        UNITS = [("dkv", b) for b in ORDER] + [("qa", b) for b in (1, 2)]
        UNITS += [("cv", c) for c in range(8)] + [("q", i) for i in range(8)] + [("v", i) for i in range(6)]
        UNITS += [("cv", 8 + c) for c in range(NX)] + [("z", c) for c in range(NX)] + [("g", c) for c in range(16)]
        U = {key: u for u, key in enumerate(UNITS)}

        def slab(name):
            i = SLAB[name]
            s = (i % NSLOT) * SLOT
            return ring[:, s:s + SLABS[i][1]]

        w1_sb = [ring[:, s * SLOT + o:s * SLOT + o + 2048] for s, o in W1_AT]
        w2_sb = [ring[:, s * SLOT + o:s * SLOT + o + 2048].rearrange("p (j n) -> p j n", j=2) for s, o in W2_AT]
        used = {"dkv": (proj_done, U["dkv", ORDER[-1]] + 1), "qa": (proj_done, U["qa", 2] + 1), "B": (proj_done, U["cv", 3] + 1),
                "C": (proj_done, U["cv", 7] + 1), "uq0": (proj_done, U["q", 3] + 1), "uq1": (proj_done, U["q", 7] + 1),
                "ukv": (qk_done, MH)}
        for i in range(4):
            used[f"xs{i}"] = (proj_done, U["cv", 8 + 4 * i + 3] + 1)
            used[f"z{i}"] = (proj_done, U["z", 4 * i + 3] + 1)
            used[f"g{i}"] = (proj_done, U["g", 4 * i + 3] + 1)
            used[f"so{i}"] = (out_done, KD + 2 * (i + 1))
        for i in range(2):
            used[f"wo{i}"] = (out_done, 4 * (i + 1))
            used[f"wout{i}"] = (wout_done, 3 + i)
        last_in_slot = {i % NSLOT: name for i, (name, _) in enumerate(SLABS)}

        block = ctx.enter_context(nc.Block())

        @block.sync
        def _(sp):
            sp.dma_start(xtok[:, 1, :], x[0:P, :]).then_inc(x_in[1], 16)
            sp.dma_start(xtok[:, 2, :], x[P:2 * P, :]).then_inc(x_in[2], 16)
            sp.dma_start(vec[:, :], vecs).then_inc(vec_in, 16)
            sp.wait_ge(meta_zero, 1)
            sp.dma_start(xtok[T0:P, 0, :], meta).then_inc(x_in[0], 16)
            for i, (name, n) in enumerate(SLABS):
                if i >= NSLOT:
                    sp.wait_ge(*used[SLABS[i - NSLOT][0]])
                sp.dma_start(slab(name), slabs[:, OFF[i]:OFF[i] + n]).then_inc(slab_in[i % NSLOT], 16)

            def load_expert(e, before):
                for k in range(len(W1_AT)):
                    if k < len(W1_AT) - 1:
                        sp.wait_ge(chunk_used, before * (CHUNKS - 2) + k + 1)
                    else:
                        sp.wait_ge(up_done, before + 1)
                    sp.dma_start(w1_sb[k], w1[bass.ds(e * D + k * P, P), :]).then_inc(w1_in[k], 16)
                for j in range(len(W2_AT)):
                    if j < len(W2_AT) - 1:
                        sp.wait_ge(chunk_used, before * (CHUNKS - 2) + len(W1_AT) + j)
                    else:
                        sp.wait_ge(down_done, before + 1)
                    sp.dma_start(w2_sb[j], w2[bass.ds(e * DE + 2 * j * P, 2 * P), :].rearrange("(j p) n -> p j n", j=2)).then_inc(w2_in[j], 16)

            for s in (3, 4, 5, 0, 1, 2):
                sp.wait_ge(*used[last_in_slot[s]])
                for k, (ks, _) in enumerate(W1_AT):
                    if ks == s:
                        sp.dma_start(w1_sb[k], w1[k * P:(k + 1) * P, :]).then_inc(w1_in[k], 16)
                for j, (js, _) in enumerate(W2_AT):
                    if js == s:
                        sp.dma_start(w2_sb[j], w2[2 * j * P:2 * (j + 1) * P, :].rearrange("(j p) n -> p j n", j=2)).then_inc(w2_in[j], 16)
            with sp.Fori(1, E) as e:
                load_expert(e, e - 1)
            sp.wait_ge(count_ready, 1)
            cm = sp.value_load(cmax_i[0:1, 0:1], min_val=0, max_val=SEQ)
            with sp.If(cm > SLOTS):
                with sp.Fori(1, SEQ // SLOTS) as r:
                    with sp.Fori(0, E) as e:
                        load_expert(e, r * E + e - 1)
            for b in range(2):
                sp.wait_ge(y_ready, b + 1)
                sp.dma_start(out[b * P:(b + 1) * P, :], fin[:, b, :]).then_inc(y_out, 16)
            sp.wait_ge(y_out, 32)

        @block.gpsimd
        def _(pool):
            steps = 0

            def link(ins):
                nonlocal steps
                steps += 1
                ins.then_inc(pool_step, 1)
                pool.wait_ge(pool_step, steps)

            pool.memset(xtok[:, 0, :], 0.0).then_inc(meta_zero, 1)
            link(pool.memset(ident[:, :], 0.0))
            pool.affine_select(out=ident[:, :], in_=ident[:, :], pattern=[[-1, P]], compare_op=ALU.not_equal, fill=1.0,
                               base=0, channel_multiplier=1).then_inc(consts_ready, 1)
            pool.memset(xraw[:, :, 0:3], 0.0).then_inc(zeros_ready, 1)
            link(pool.memset(ones[:, :], 1.0))
            link(pool.memset(tri[:, :], 1.0))
            link(pool.affine_select(out=tri[:, 0:P], in_=tri[:, 0:P], pattern=[[1, P]], compare_op=ALU.is_ge, fill=0.0,
                                    base=0, channel_multiplier=-1))
            link(pool.memset(metarows[:, :], 1.0))
            link(pool.affine_select(out=metarows[:, :], in_=metarows[:, :], pattern=[[0, 2 * P]], compare_op=ALU.is_ge,
                                    fill=0.0, base=-T0, channel_multiplier=1))
            link(pool.affine_select(out=trimeta[:, :], in_=tri[:, 0:P], pattern=[[0, P]], compare_op=ALU.is_ge,
                                    fill=0.0, base=-T0, channel_multiplier=1))
            link(pool.memset(keymask[:, :], 0.0))
            link(pool.affine_select(out=keymask[:, L - P:L], in_=keymask[:, L - P:L], pattern=[[-1, P]],
                                    compare_op=ALU.is_ge, fill=NEG, base=0, channel_multiplier=1))
            link(pool.iota(iota_slot[:, :], pattern=[[1, SLOTS]], base=0, channel_multiplier=0,
                           allow_small_or_imprecise_dtypes=True))
            link(pool.iota(iota_e[:, :], pattern=[[1, E]], base=0, channel_multiplier=0,
                           allow_small_or_imprecise_dtypes=True))
            link(pool.memset(AT[:, :], 0.0))
            link(pool.memset(probs[:, :, :, 0:T0], 0.0))
            pool.memset(BT[:, :, 0:T0], 0.0).then_inc(consts_ready, 1)
            pool.wait_ge(q_roped, 1)
            pool.memset(xT[:, :, 0:T0], 0.0).then_inc(zeros_ready, 1)
            pool.wait_ge(ssdy_done, NX)
            pool.dma_start(xres[:, 0, :], x[0:P, :]).then_inc(xres_in, 16)
            pool.dma_start(xres[:, 1, :], x[P:2 * P, :]).then_inc(xres_in, 16)
            pool.memset(PW[:, :, :], -1.0).then_inc(moe_zero, 1)
            pool.wait_ge(proj_done, len(UNITS))
            pool.memset(w(0, 3072), 0.0).then_inc(moe_zero, 1)
            pool.wait_ge(moe_zero, 2)
            pool.dma_start(b1all[0:E, :], b1).then_inc(bias_in, 16)
            pool.dma_start(b2all[0:E, :], b2).then_inc(bias_in, 16)
            pool.wait_ge(out_done, KD)
            pool.dma_start(w(11776, 2048), rows).then_inc(rows_in, 16)
            pool.wait_ge(merged, 2 * KD)
            pool.memset(wpad[:, :, :], 0.0).then_inc(moe_zero, 1)
            pool.memset(ob[:, :], 0.0).then_inc(ob_ready, 1)
            pool.memset(actT[:, :, :], 0.0).then_inc(actT_ready, 1)
            for b in range(2):
                if b == 1:
                    pool.wait_ge(wout_done, 4)
                    pool.memset(scat[:, :, :], 0.0).then_inc(scat_ready, 1)
                pool.wait_ge(rsn_ready, b + 1)
                pool.wait_ge(xn_trans, 2 * (b + 1))
                pool.tensor_scalar(xn[:, b, :], xn[:, b, :], rsn[:, b:b + 1], None, ALU.mult).then_inc(xn_scaled, 1)

        @block.scalar
        def _(a):
            for b in ORDER:
                a.wait_ge(x_in[b], 16)
                a.activation(junk[:, b, :], xtok[:, b, :], ACT.Square, accum_out=ssx[:, b:b + 1]).then_inc(x_squared, 1)

            def unit(kind, i):
                u = U[kind, i]
                a.wait_ge(proj_done, u + 1)
                return bank[u % 2]

            for b in ORDER:
                ps = unit("dkv", b)
                a.activation(junk2[:, b * KVL:(b + 1) * KVL], ps[:, HEADS_S:HEADS_S + KVL], ACT.Square, accum_out=ssk[:, b:b + 1])
                a.activation(mid[:, b, :], ps[:, 0:DKV], ACT.Copy).then_inc(proj_read, 1)
            for b in range(2):
                ps = unit("qa", b + 1)
                a.activation(junk2[:, 768 + b * QL:768 + (b + 1) * QL], ps[:, 0:QL], ACT.Square, accum_out=ssq[:, b:b + 1])
                a.activation(qa[:, b, :], ps[:, 0:QL], ACT.Copy).then_inc(proj_read, 1)

            def conv_in(c):
                ps = unit("cv", c)
                if c == 0:
                    a.wait_ge(zeros_ready, 1)
                if c >= 2:
                    a.wait_ge(conv_done, c - 1)
                a.activation(xraw[:, c % 2, 3:3 + L], ps[:, 0:L], ACT.Copy).then_inc(proj_read, 1)

            def tanh_of(c):
                a.wait_ge(conv_done, c + 1)
                if c >= 2:
                    a.wait_ge(conv_fin, c - 1)
                a.activation(convt[:, c % 2, :], conv[:, c % 2, :], ACT.Tanh).then_inc(conv_tanh, 1)

            for c in range(4):
                conv_in(c)
                if c:
                    tanh_of(c - 1)
            tanh_of(3)
            a.wait_ge(dt_abs, 1)
            a.activation(dt[:, :], dta[:, :], ACT.Exp, scale=-1.0).then_inc(act_step, 1)
            a.activation(negA[:, :], v("a_log"), ACT.Exp).then_inc(act_step, 1)
            a.wait_ge(act_step, 2)
            a.activation(dta[:, :], dt[:, :], ACT.Ln, bias=1.0).then_inc(dt_ln, 1)
            a.wait_ge(latent_trans, 1)
            for i in range(2):
                a.activation(kTh[NOPE:QH, i, :], bank[7][NOPE:QH, T0:T], ACT.Copy).then_inc(kpeT_ready, 1)
            for c in range(4, 8):
                conv_in(c)
                if c > 4:
                    tanh_of(c - 1)
            tanh_of(7)
            for i in range(8):
                ps = unit("q", i)
                b, part = i % 2, i // 2
                a.activation(q_sb[:, b, part * QL:(part + 1) * QL], ps[:, 0:QL], ACT.Copy,
                             scale=float(QH) ** -0.5).then_inc(proj_read, 1)
            a.wait_ge(dA_ready, 1)
            for i in range(6):
                ps = unit("v", i)
                a.activation(V[:, i // 2, (i % 2) * 512:(i % 2 + 1) * 512], ps[:, :], ACT.Copy).then_inc(proj_read, 1)

            def k_head(h):
                a.wait_ge(qk_done, h + 1)
                a.activation(kTh[0:NOPE, h % 2, :], bank[6][0:NOPE, 0:L], ACT.Copy).then_inc(kT_ready, 1)

            def exp_head(h):
                a.wait_ge(scores_read, h + 1)
                a.activation(probs[:, h % 2, 0, T0:2 * P], probs[:, h % 2, 0, T0:2 * P], ACT.Exp,
                             bias=nmax[:, h % 2, 0:1], accum_out=rsum[:, h % 2, 0:1])
                a.activation(probs[:, h % 2, 1, T0:T], probs[:, h % 2, 1, T0:T], ACT.Exp,
                             bias=nmax[:, h % 2, 1:2], accum_out=rsum[:, h % 2, 1:2]).then_inc(exp_done, 1)

            k_head(0)
            exp_head(0)
            for h in range(MH):
                if h + 1 < MH:
                    k_head(h + 1)
                conv_in(8 + h)
                if h:
                    tanh_of(8 + h - 1)
                if h and h % 2 == 0:
                    a.wait_ge(pv_done, h)
                    a.activation(attnT[:, h // 2 - 1, :], bank[5][:, P:3 * P], ACT.Copy).then_inc(pv_read, 1)
                if h + 1 < MH:
                    exp_head(h + 1)
                a.wait_ge(pT_done, h + 1)
                a.activation(pT[:, 0:512], bank[4][:, :], ACT.Copy).then_inc(pTa_ready, 1)
            tanh_of(8 + MH - 1)
            a.wait_ge(pv_done, MH)
            a.activation(attnT[:, KD - 1, :], bank[5][:, P:3 * P], ACT.Copy).then_inc(pv_read, 1)

            def exp_decay(c):
                a.wait_ge(diff_ready, c + 1)
                a.activation(decay[:, c % 2, :, :], decay[:, c % 2, :, :], ACT.Exp).then_inc(decay_exp, 1)

            exp_decay(0)
            for c in range(NX):
                if c + 1 < NX:
                    exp_decay(c + 1)
                ps = unit("z", c)
                if c >= 2:
                    a.wait_ge(y2_ready, c - 1)
                a.activation(ztanh[:, c % 2, :], ps[:, 0:SEQ], ACT.Tanh, scale=0.5)
                a.activation(zcopy[:, c % 2, :], ps[:, 0:SEQ], ACT.Copy).then_inc(proj_read, 1)
                a.wait_ge(y2_ready, c + 1)
                if c >= 2:
                    a.wait_ge(gsum_done, c - 1)
                a.activation(ysq[:, c % 2, :], y2T[:, c, :], ACT.Square, scale=0.5).then_inc(ysq_ready, 1)
            for c in range(16):
                ps = unit("g", c)
                a.activation(gt[:, c, :], ps[:, 0:SEQ], ACT.Tanh, scale=0.5).then_inc(proj_read, 1)
            def square_half(b, n):
                a.wait_ge(h1_ready, 2 * b + n + 1)
                a.activation(hsq[:, 2 * b + n, :], h1[:, b, n * 512:(n + 1) * 512], ACT.Square,
                             accum_out=ssh4[:, b, n:n + 1]).then_inc(h1_squared, 1)

            def xn_copy(b, n):
                a.wait_ge(xn_trans, 2 * b + n + 1)
                a.activation(xnT[:, b, 4 * n:4 * n + 4, :].rearrange("p k t -> p (k t)"), bank[2 * b + n][:, :],
                             ACT.Copy).then_inc(xnT_ready, 1)

            def top_weights(b):
                a.wait_ge(top_ready, b + 1)
                a.activation(e4[:, b, :], mx8[:, b, 0:TOPK], ACT.Exp, bias=nm4[:, b:b + 1],
                             accum_out=s4[:, b:b + 1]).then_inc(top_exp, 1)

            square_half(0, 0)
            square_half(0, 1)
            xn_copy(0, 0)
            square_half(1, 0)
            xn_copy(0, 1)
            top_weights(0)
            square_half(1, 1)
            xn_copy(1, 0)
            xn_copy(1, 1)
            top_weights(1)
            a.wait_ge(w_trans, 1)
            a.activation(wTs[:, :], bank[5][:, 0:SEQ], ACT.Copy).then_inc(wT_ready, 1)

            def gathered(n):
                a.wait_ge(gather_done, n)
                a.activation(xg[:, :], bank[7][:, :], ACT.Copy).then_inc(xg_ready, 1)

            def gatheredT(n):
                a.wait_ge(xg_trans, n)
                a.activation(xgT[:, :, :].rearrange("p j t -> p (j t)"), bank[7][:, :], ACT.Copy).then_inc(xgT_ready, 1)

            def expert_round(r):
                gathered(r * (E + 1) + 1)
                gatheredT(r * (E + 1) + 1)
                with a.Fori(0, E) as e:
                    t, g = r * E + e, r * (E + 1) + e + 2
                    a.wait_ge(glu_ready, t + 1)
                    a.activation(sig[:, :], glu[:, :], ACT.Tanh, scale=0.5 * ALPHA).then_inc(sig_ready, 1)
                    gathered(g)
                    gatheredT(g)
                    a.wait_ge(act_trans, t + 1)
                    a.activation(actT[:, :, :].rearrange("p j t -> p (j t)"), bank[4][:, :], ACT.Copy,
                                 scale=0.5).then_inc(actT_ready, 1)
                    a.wait_ge(down_done, t + 1)
                    a.activation(ob[:, :], bank[6][:, :], ACT.Copy).then_inc(ob_ready, 1)

            expert_round(0)
            a.wait_ge(count_ready, 1)
            cm = a.value_load(cmax_i[0:1, 0:1], min_val=0, max_val=SEQ)
            with a.If(cm > SLOTS):
                with a.Fori(1, SEQ // SLOTS) as r:
                    expert_round(r)
            for b in range(2):
                a.wait_ge(h2_ready, b + 1)
                a.activation(w((3072, 9216)[b], 1024), h1[:, b, :], ACT.Square, accum_out=ssh[:, b:b + 1]).then_inc(h2_squared, 1)

        @block.vector
        def _(d):
            steps = 0

            def link(ins):
                nonlocal steps
                steps += 1
                ins.then_inc(dve_step, 1)
                d.wait_ge(dve_step, steps)

            def rsqrt(y, val, tmp):
                yi = y.bitcast(I32)
                link(d.tensor_scalar(yi, val.bitcast(I32), 1, None, ALU.logical_shift_right))
                link(d.tensor_scalar(yi, yi, -1.0, 1597463007.0, ALU.mult, ALU.add))
                for _ in range(3):
                    link(d.tensor_tensor(tmp, y, y, ALU.mult))
                    link(d.scalar_tensor_tensor(tmp, val, -0.5, tmp, ALU.mult, ALU.mult))
                    link(d.scalar_tensor_tensor(y, tmp, 1.5, y, ALU.add, ALU.mult))

            def rstd(dst, src, n, eps):
                cols = src.shape[1]
                link(d.tensor_scalar(src, src, 1.0 / n, eps, ALU.mult, ALU.add))
                rsqrt(dst, src, nrt[:, 0:cols])


            for i, b in enumerate(ORDER):
                d.wait_ge(x_squared, i + 1)
                rstd(rsx[:, b:b + 1], ssx[:, b:b + 1], D, EPS)
                d.tensor_scalar(xtok[:, b, :], xtok[:, b, :], rsx[:, b:b + 1], None, ALU.mult).then_inc(hn_ready, 1)
            d.wait_ge(vec_in, 16)
            for i in range(6):
                b, k = ORDER[i // 2], 4 * (i % 2)
                d.wait_ge(hn_trans, i + 1)
                d.tensor_tensor(hnT[:, k:k + 4, b * P:(b + 1) * P], bank[i][:, :].rearrange("p (k t) -> p k t", k=4),
                                v("norm_mix", k, 4).unsqueeze(2).to_broadcast([P, 4, P]), ALU.mult).then_inc(hnT_ready, 1)
            link(d.tensor_scalar(v("conv_w"), v("conv_w"), 0.5, None, ALU.mult))
            link(d.tensor_scalar(v("conv_b"), v("conv_b"), 0.5, None, ALU.mult))
            link(d.tensor_scalar(v("ssd_norm"), v("ssd_norm"), 0.5, None, ALU.mult))
            d.wait_ge(proj_read, 3)
            rstd(rsk, ssk, KVL, MLA_EPS)
            for b in range(NB):
                d.tensor_scalar(ckk[:, b, 0:KVL], mid[:, b, HEADS_S:HEADS_S + KVL], rsk[:, b:b + 1], None, ALU.mult)
            d.memset(ckk[:, :, KVL:KVL + NOPE], 0.0)
            k1, k2 = mid[:, :, HEADS_S + KVL:HEADS_S + KVL + 16], mid[:, :, HEADS_S + KVL + 16:DKV]
            cosv = v("cos").rearrange("p (b r) -> p b r", b=NB)
            sinv = v("sin").rearrange("p (b r) -> p b r", b=NB)
            d.tensor_tensor(kr[:, 0], k1, cosv, ALU.mult)
            d.tensor_tensor(kr[:, 1], k2, sinv, ALU.mult)
            d.tensor_tensor(kr[:, 2], k2, cosv, ALU.mult)
            link(d.tensor_tensor(kr[:, 3], k1, sinv, ALU.mult))
            d.tensor_tensor(ckk[:, :, KVL + NOPE:KVL + NOPE + 16], kr[:, 0], kr[:, 1], ALU.subtract)
            d.tensor_tensor(ckk[:, :, KVL + NOPE + 16:KVL + QH], kr[:, 2], kr[:, 3], ALU.add)
            dt3 = dtv.rearrange("p (b h) -> p b h", b=NB)
            link(d.tensor_tensor(dt3, mid[:, :, 0:HEADS_S], v("dt_bias").unsqueeze(1).to_broadcast([P, NB, HEADS_S]), ALU.add))
            d.scalar_tensor_tensor(dta[:, :], dtv[:, :], -1.0, dtv[:, :], ALU.mult, ALU.max).then_inc(dt_abs, 1)
            d.wait_ge(proj_read, 5)
            rstd(rsq, ssq, QL, MLA_EPS)
            for b in range(2):
                last = d.tensor_scalar(qa[:, b, :], qa[:, b, :], rsq[:, b:b + 1], None, ALU.mult)
            last.then_inc(latent_ready, 1)

            def conv_of(c):
                d.wait_ge(proj_read, U["cv", c] + 1)
                if c >= 2:
                    d.wait_ge(conv_fin, c - 1)
                dst, src = conv[:, c % 2, :], xraw[:, c % 2, :]
                link(d.tensor_scalar(dst, src[:, 3:3 + L], v("conv_w", 4 * c + 3, 1), v("conv_b", c, 1), ALU.mult, ALU.add))
                for j in (0, 1):
                    link(d.scalar_tensor_tensor(dst, src[:, j:j + L], v("conv_w", 4 * c + j, 1), dst, ALU.mult, ALU.add))
                d.scalar_tensor_tensor(dst, src[:, 2:2 + L], v("conv_w", 4 * c + 2, 1), dst, ALU.mult,
                                       ALU.add).then_inc(conv_done, 1)

            def silu_of(c):
                d.wait_ge(conv_tanh, c + 1)
                at = slice(NMETA, L) if 4 <= c < 8 else slice(0, L)
                dst = BT[:, c, T0:T] if c < 4 else CT[:, c - 4, :] if c < 8 else xT[:, c - 8, T0:T]
                d.scalar_tensor_tensor(dst, convt[:, c % 2, at], 1.0, conv[:, c % 2, at], ALU.add,
                                       ALU.mult).then_inc(conv_fin, 1)

            d.wait_ge(consts_ready, 2)
            for c in range(4):
                conv_of(c)
                if c:
                    silu_of(c - 1)
            silu_of(3)
            d.wait_ge(latent_trans, 1)
            for k in range(KKV):
                d.tensor_scalar(ckvT[:, k, :], bank[5 + k][:, 0:T], v("kv_norm", k, 1), None, ALU.mult)
            for k in range(KQ):
                last = d.tensor_scalar(qaT[:, k, :], bank[3 + k // 2][:, (k % 2) * SEQ:(k % 2 + 1) * SEQ],
                                       v("q_norm", k, 1), None, ALU.mult)
            last.then_inc(latentT_ready, 1)
            d.wait_ge(dt_ln, 1)
            link(d.scalar_tensor_tensor(dt[:, :], dtv[:, :], 0.0, dta[:, :], ALU.max, ALU.add))
            d.scalar_tensor_tensor(dA.rearrange("p (b h) -> p b h", b=NB), dt.rearrange("p (b h) -> p b h", b=NB), -1.0,
                                   negA[:, :].unsqueeze(1).to_broadcast([P, NB, HEADS_S]), ALU.mult,
                                   ALU.mult).then_inc(dA_ready, 1)
            for c in range(4, 8):
                conv_of(c)
                if c > 4:
                    silu_of(c - 1)
            silu_of(7)
            d.wait_ge(cum_done, 1)
            d.tensor_copy(AT[0:HEADS_S, :], bank[2][0:HEADS_S, 0:SEQ])
            d.tensor_copy(As[:, :], bank[3][:, 0:NB * HEADS_S]).then_inc(cum_read, 1)
            d.wait_ge(proj_read, U["q", 7] + 1)
            for b in range(2):
                qv = q_sb[:, b, :].rearrange("p (h r) -> p h r", h=MH)
                q1, q2 = qv[:, :, NOPE:NOPE + 16], qv[:, :, NOPE + 16:QH]
                cb = cosv[:, b + 1, :].unsqueeze(1).to_broadcast([P, MH, 16])
                sb_ = sinv[:, b + 1, :].unsqueeze(1).to_broadcast([P, MH, 16])
                o = 4 * b
                d.tensor_tensor(ropet[:, o], q1, cb, ALU.mult)
                d.tensor_tensor(ropet[:, o + 1], q2, sb_, ALU.mult)
                d.tensor_tensor(ropet[:, o + 2], q2, cb, ALU.mult)
                link(d.tensor_tensor(ropet[:, o + 3], q1, sb_, ALU.mult))
                d.tensor_tensor(q1, ropet[:, o], ropet[:, o + 1], ALU.subtract)
                last = d.tensor_tensor(q2, ropet[:, o + 2], ropet[:, o + 3], ALU.add)
            last.then_inc(q_roped, 1)

            def q_head(h):
                d.wait_ge(qk_done, h + 1)
                d.tensor_copy(qTh[0:QH, h % 2, :], bank[7][0:QH, 0:SEQ]).then_inc(qT_ready, 1)

            def max_head(h):
                d.wait_ge(scores_done, h + 1)
                if h >= 2:
                    d.wait_ge(pT_done, h - 1)
                d.tensor_tensor_reduce(out=probs[:, h % 2, 0, T0:2 * P], in0=bank[2][:, 0:L - P], in1=keymask[:, P:L],
                                       scale=1.0, scalar=NEG, op0=ALU.add, op1=ALU.max, accum_out=rmax[:, 0:1])
                link(d.tensor_tensor_reduce(out=probs[:, h % 2, 1, T0:T], in0=bank[3][:, 0:L], in1=keymask[:, :],
                                            scale=1.0, scalar=NEG, op0=ALU.add, op1=ALU.max, accum_out=rmax[:, 1:2]))
                d.tensor_scalar(nmax[:, h % 2, :], rmax[:, :], -1.0, None, ALU.mult).then_inc(scores_read, 1)

            def norm_head(h):
                d.wait_ge(exp_done, h + 1)
                link(d.reciprocal(rinv[:, :], rsum[:, h % 2, :]))
                d.tensor_scalar(probs[:, h % 2, 0, T0:2 * P], probs[:, h % 2, 0, T0:2 * P], rinv[:, 0:1], None, ALU.mult)
                d.tensor_scalar(probs[:, h % 2, 1, T0:T], probs[:, h % 2, 1, T0:T], rinv[:, 1:2], None,
                                ALU.mult).then_inc(probs_ready, 1)

            q_head(0)
            max_head(0)
            d.wait_ge(zeros_ready, 2)
            for h in range(MH):
                if h + 1 < MH:
                    q_head(h + 1)
                norm_head(h)
                conv_of(8 + h)
                if h:
                    silu_of(8 + h - 1)
                if h + 1 < MH:
                    max_head(h + 1)
                d.wait_ge(pT_done, h + 1)
                d.tensor_copy(pT[:, 512:640], bank[5][:, 0:P]).then_inc(pTb_ready, 1)
            silu_of(8 + MH - 1)
            for g in range(GROUPS):
                d.wait_ge(cb_done, g + 1)
                ba, bb = bank[4 + 2 * (g % 2)], bank[5 + 2 * (g % 2)]
                d.tensor_copy(CBm[:, g, 0:SEQ], ba[:, 0:SEQ])
                d.tensor_tensor(CBm[:, g, SEQ:2 * SEQ], ba[:, SEQ:2 * SEQ], tri[:, :], ALU.mult)
                d.tensor_tensor(CBm[:, g, 2 * SEQ:2 * SEQ + P], bb[:, 0:P], tri[:, 0:P], ALU.mult).then_inc(cb_read, 1)

            def diff_of(c):
                d.wait_ge(acum_done, c + 1)
                for j in range(2):
                    h = 2 * c + j
                    src = bank[2][:, j * SEQ:(j + 1) * SEQ]
                    for b, (lo, at) in enumerate([(0, 0), (0, SEQ), (P, 2 * SEQ)]):
                        col = b * HEADS_S + h
                        last = d.tensor_scalar(decay[:, c % 2, j, at:at + SEQ - lo], src[:, lo:SEQ], As[:, col:col + 1],
                                               0.0, ALU.subtract, ALU.min)
                last.then_inc(diff_ready, 1)

            def xdt_of(c):
                d.wait_ge(xtr_done, c + 1)
                d.tensor_tensor(xdt[:, c % 2, :, :].rearrange("p b (j t) -> p b j t", j=2),
                                bank[6][:, 0:T].rearrange("p (b j t) -> p b j t", b=NB, j=2),
                                dt.rearrange("p (b h) -> p b h", b=NB)[:, :, 2 * c:2 * c + 2].unsqueeze(3)
                                .to_broadcast([P, NB, 2, VH]), ALU.mult).then_inc(xdt_ready, 1)

            def sc_of(c):
                d.wait_ge(decay_exp, c + 1)
                d.tensor_tensor(decay[:, c % 2, :, :], decay[:, c % 2, :, :],
                                CBm[:, c // CHUNKS_PER_GROUP, :].unsqueeze(1).to_broadcast([P, 2, 640]),
                                ALU.mult).then_inc(sc_ready, 1)

            def var_group(g):
                d.wait_ge(gsum_done, CHUNKS_PER_GROUP * (g + 1))
                d.tensor_scalar(var_g[:, g * SEQ:(g + 1) * SEQ], bank[7][:, 0:SEQ], 1.0 / 512, EPS, ALU.mult,
                                ALU.add).then_inc(gsum_read, 1)

            diff_of(0)
            xdt_of(0)
            sc_of(0)
            for c in range(NX):
                if c + 1 < NX:
                    diff_of(c + 1)
                    xdt_of(c + 1)
                d.wait_ge(proj_read, U["z", c] + 1)
                d.scalar_tensor_tensor(zw, ztanh[:, c % 2, :], 1.0, zcopy[:, c % 2, :], ALU.add, ALU.mult)
                if c + 1 < NX:
                    sc_of(c + 1)
                d.wait_ge(ssdy_done, c + 1)
                d.scalar_tensor_tensor(yv, xT[:, c, P:T], v("d_skip", c, 1), bank[3][:, 0:SEQ], ALU.mult,
                                       ALU.add).then_inc(ssdy_read, 1)
                d.wait_ge(ssdy_read, c + 1)
                d.tensor_tensor(y2T[:, c, :], yv, zw, ALU.mult).then_inc(y2_ready, 1)
                if c and c % CHUNKS_PER_GROUP == 0:
                    var_group(c // CHUNKS_PER_GROUP - 1)
            var_group(GROUPS - 1)
            d.wait_ge(gsum_read, GROUPS)
            rsqrt(rstd_g, var_g, tmp_g)
            for c in range(NX):
                g = c // CHUNKS_PER_GROUP
                d.scalar_tensor_tensor(y2T[:, c, :], y2T[:, c, :], v("ssd_norm", c, 1), rstd_g[:, g * SEQ:(g + 1) * SEQ],
                                       ALU.mult, ALU.mult).then_inc(yn_ready, 1)
            d.wait_ge(proj_read, len(UNITS))
            for m in range(KD):
                d.wait_ge(out_done, m + 1)
                d.scalar_tensor_tensor(mT[:, m, :], gt[:, KD + m, :], 1.0, bank[2 + m % 2][:, 0:SEQ], ALU.add,
                                       ALU.mult).then_inc(merged, 1)
            for m in range(KD):
                d.wait_ge(out_done, KD + m + 1)
                link(d.scalar_tensor_tensor(mtmp[:, m % 2, :], gt[:, m, :], 1.0, bank[2 + m % 2][:, 0:SEQ], ALU.add, ALU.mult))
                d.tensor_tensor(mT[:, m, :], mT[:, m, :], mtmp[:, m % 2, :], ALU.add).then_inc(merged, 1)
            d.wait_ge(xres_in, 32)
            d.wait_ge(rows_in, 16)

            def residual_half(b, n):
                d.wait_ge(wout_done, 2 * b + n + 1)
                half = slice(n * 512, (n + 1) * 512)
                d.scalar_tensor_tensor(h1[:, b, half], bank[4 + 2 * n + b][:, :], 0.5, xres[:, b, half], ALU.mult,
                                       ALU.add).then_inc(h1_ready, 1)
                d.wait_ge(h1_ready, 2 * b + n + 1)
                d.tensor_tensor(xn[:, b, half], h1[:, b, half], nf[:, half], ALU.mult).then_inc(xn_ready, 1)

            def rstd_block(b):
                d.wait_ge(h1_squared, 2 * (b + 1))
                link(d.tensor_tensor(ssh[:, b:b + 1], ssh4[:, b, 0:1], ssh4[:, b, 1:2], ALU.add))
                rstd(rsh[:, b:b + 1], ssh[:, b:b + 1], D, EPS)
                d.tensor_copy(rsn[:, b:b + 1], rsh[:, b:b + 1]).then_inc(rsn_ready, 1)

            def top4(b):
                d.wait_ge(logits_done, b + 1)
                link(d.scalar_tensor_tensor(lg[:, b, :], bank[4 + b][:, 0:E], rsh[:, b:b + 1], v("b_router"), ALU.mult, ALU.add))
                link(d.max(mx8[:, b, :], lg[:, b, :]))
                link(d.max_index(idx[:, 8 * b:8 * b + 8], mx8[:, b, :], lg[:, b, :]))
                d.tensor_scalar(nm4[:, b:b + 1], mx8[:, b, 0:1], -1.0, None, ALU.mult).then_inc(top_ready, 1)
                link(d.tensor_copy(idxf[:, b, :], idx[:, 8 * b:8 * b + 8]))
                link(d.tensor_tensor(chosen[:, b, :, :], iota_e[:, :].unsqueeze(1).to_broadcast([P, TOPK, E]),
                                     idxf[:, b, 0:TOPK].unsqueeze(2).to_broadcast([P, TOPK, E]), ALU.is_equal))
                d.tensor_reduce(mask[:, b, :], chosen[:, b, :, :].rearrange("p j e -> p e j"), AX.X, ALU.add).then_inc(mask_ready, 1)

            def weights(b):
                d.wait_ge(top_exp, b + 1)
                link(d.reciprocal(r4[:, b:b + 1], s4[:, b:b + 1]))
                link(d.tensor_scalar(e4[:, b, :], e4[:, b, :], r4[:, b:b + 1], None, ALU.mult))
                link(d.tensor_tensor(chosen[:, b, :, :], chosen[:, b, :, :],
                                     e4[:, b, :].unsqueeze(2).to_broadcast([P, TOPK, E]), ALU.mult))
                link(d.tensor_reduce(PW[:, 2 + b, 0:E], chosen[:, b, :, :].rearrange("p j e -> p e j"), AX.X, ALU.add))

            residual_half(0, 0)
            residual_half(0, 1)
            rstd_block(0)
            residual_half(1, 0)
            d.wait_ge(moe_zero, 3)
            top4(0)
            residual_half(1, 1)
            rstd_block(1)
            weights(0)
            top4(1)
            weights(1)
            d.tensor_copy(wpad[:, :, 0:E], PW[:, 2:4, 0:E]).then_inc(route_ready, 1)
            d.wait_ge(pos_done, 1)
            ps = bank[6][:, 0:2 * E].rearrange("p (b e) -> p b e", b=2)
            link(d.tensor_tensor(PW[:, 0:2, 0:E], ps, mask[:, :, :], ALU.mult))
            link(d.tensor_scalar(PW[:, 0:2, 0:E], PW[:, 0:2, 0:E], -1.0, None, ALU.add))

            def count():
                link(d.tensor_reduce(cmax[:, :], bank[6][:, 2 * E:3 * E], AX.X, ALU.max))
                d.tensor_copy(cmax_i[:, :], cmax[:, :]).then_inc(count_ready, 1)

            PER_EXPERT = 2
            PER_ROUND = 1 + E * PER_EXPERT + 1

            def expert_round(r, first):
                def link_at(n):
                    def link(ins):
                        nonlocal n
                        n = n + 1
                        ins.then_inc(moe_step, 1)
                        d.wait_ge(moe_step, n)
                    return link

                def pick(e, link, gathers):
                    link(d.tensor_copy(pw[:, :], PW[:, :, bass.ds(e, 1)].rearrange("p i o -> p (i o)")))
                    if gathers is not None:
                        d.wait_ge(gather_done, gathers)
                    d.tensor_scalar(hot[:, 0, :], iota_slot[:, :], pw[:, 0:1], None, ALU.is_equal)
                    d.tensor_scalar(hot[:, 1, :], iota_slot[:, :], pw[:, 1:2], None, ALU.is_equal).then_inc(hot_ready, 1)

                pick(0, link_at(r * PER_ROUND), None if first else r * (E + 1))
                d.tensor_copy(bsel[:, :], ident[:, 0:1].to_broadcast([P, SLOTS])).then_inc(bsel_ready, 1)
                if first:
                    count()
                with d.Fori(0, E) as e:
                    t = r * E + e
                    link = link_at(r * PER_ROUND + 1 + e * PER_EXPERT)
                    for b in range(2):
                        last = d.tensor_scalar(hotw[:, b, :, :], iota_slot[:, :].unsqueeze(1).to_broadcast([P, 2, SLOTS]),
                                               pw[:, b:b + 1], pw[:, 2 + b:3 + b], ALU.is_equal, ALU.mult)
                    last.then_inc(hotw_ready, 1)
                    d.wait_ge(hotw_ready, t + 1)
                    pick(e + 1, link, r * (E + 1) + e + 1)
                    d.wait_ge(up_done, t + 1)
                    for i in range(2):
                        hv = bank[4 + i][:, :].rearrange("p (f o) -> p f o", o=2)
                        last = d.tensor_scalar(glu[:, i * 256:(i + 1) * 256], hv[:, :, 0], LIMIT, None, ALU.min)
                    last.then_inc(glu_ready, 1)
                    for i in range(2):
                        hv = bank[4 + i][:, :].rearrange("p (f o) -> p f o", o=2)
                        last = d.tensor_scalar(lin[:, i * 256:(i + 1) * 256], hv[:, :, 1], LIMIT, -LIMIT, ALU.min, ALU.max)
                    last.then_inc(up_read, 1)
                    d.tensor_copy(bsel[:, :], ident[:, bass.ds(e + 1, 1)].to_broadcast([P, SLOTS])).then_inc(bsel_ready, 1)
                    d.wait_ge(up_read, t + 1)
                    link(d.scalar_tensor_tensor(lin[:, :], lin[:, :], 1.0, glu[:, :], ALU.add, ALU.mult))
                    d.wait_ge(sig_ready, t + 1)
                    d.scalar_tensor_tensor(act[:, :], sig[:, :], 1.0, lin[:, :], ALU.add, ALU.mult).then_inc(act_ready, 1)
                    d.wait_ge(scat_trans, t + 1)
                    d.tensor_copy(scat[0:SLOTS, 0, :], bank[5][0:SLOTS, 0:SEQ])
                    d.tensor_copy(scat[SLOTS:P, 1, :], bank[5][SLOTS:P, 0:SEQ]).then_inc(scat_ready, 1)

            expert_round(0, True)
            cm = d.value_load(cmax_i[0:1, 0:1], min_val=0, max_val=SEQ)
            with d.If(cm > SLOTS):
                with d.Fori(1, SEQ // SLOTS) as r:
                    d.tensor_scalar(PW[:, 0:2, 0:E], PW[:, 0:2, 0:E], -float(SLOTS), None, ALU.add).then_inc(moe_step, 1)
                    d.wait_ge(moe_step, r * PER_ROUND)
                    expert_round(r, False)
            for b in range(2):
                d.wait_ge(scattered, b + 1)
                for n in range(2):
                    last = d.tensor_tensor(h1[:, b, n * 512:(n + 1) * 512], bank[2 * b + n][:, :],
                                           h1[:, b, n * 512:(n + 1) * 512], ALU.add)
                last.then_inc(h2_ready, 1)
            for b in range(2):
                d.wait_ge(h2_squared, b + 1)
                rstd(rsh[:, b:b + 1], ssh[:, b:b + 1], D, EPS)
                d.scalar_tensor_tensor(fin[:, b, :], h1[:, b, :], rsh[:, b:b + 1], nfin, ALU.mult, ALU.mult).then_inc(y_ready, 1)

        @block.tensor
        def _(pe):
            def mm(o, lhsT, rhs, start=True, stop=True):
                return pe.matmul(o, lhsT, rhs, start=start, stop=stop)

            arrived = [0] * NSLOT

            def take(name):
                s = SLAB[name] % NSLOT
                arrived[s] += 16
                pe.wait_ge(slab_in[s], arrived[s])
                return slab(name)

            def unit(kind, i):
                u = U[kind, i]
                if u >= 2:
                    pe.wait_ge(proj_read, u - 1)
                return bank[u % 2]

            pe.wait_ge(consts_ready, 1)
            for i in range(6):
                b, k0 = ORDER[i // 2], 4 * (i % 2)
                pe.wait_ge(hn_ready, i // 2 + 1)
                for k in range(4):
                    last = pe.transpose(bank[i][:, k * P:(k + 1) * P], xtok[:, b, (k0 + k) * P:(k0 + k + 1) * P], ident[:, :])
                last.then_inc(hn_trans, 1)
            wsl = take("dkv").rearrange("p (k n) -> p k n", k=KD)
            for i, b in enumerate(ORDER):
                pe.wait_ge(hnT_ready, 6 if i else 2)
                ps = bank[i % 2]
                if i >= 2:
                    ps = unit("dkv", b)
                for k in range(KD):
                    last = mm(ps[:, 0:DKV], hnT[:, k, b * P:(b + 1) * P], wsl[:, k, :], k == 0, k == KD - 1)
                last.then_inc(proj_done, 1)
            wsl = take("qa").rearrange("p (k n) -> p k n", k=KD)
            for b in (1, 2):
                ps = unit("qa", b)
                for k in range(KD):
                    last = mm(ps[:, 0:QL], hnT[:, k, b * P:(b + 1) * P], wsl[:, k, :], k == 0, k == KD - 1)
                last.then_inc(proj_done, 1)

            def feature_unit(kind, i, wsl, j, t0):
                ps = unit(kind, i)
                for k in range(KD):
                    last = mm(ps[:, 0:T - t0], wsl[:, k, j * P:(j + 1) * P], hnT[:, k, t0:T], k == 0, k == KD - 1)
                last.then_inc(proj_done, 1)

            wsl = take("B").rearrange("p (k n) -> p k n", k=KD)
            for c in range(4):
                feature_unit("cv", c, wsl, c, T0)
            pe.wait_ge(latent_ready, 1)
            for b in range(NB):
                for k in range(KKV):
                    pe.transpose(bank[5 + k][:, b * P:(b + 1) * P], ckk[:, b, k * P:(k + 1) * P], ident[:, :])
                pe.transpose(bank[7][0:QH, b * P:(b + 1) * P], ckk[:, b, KVL:KVL + QH], ident[:, :])
            for b in range(2):
                for k in range(KQ):
                    last = pe.transpose(bank[3 + k // 2][:, (k % 2) * SEQ + b * P:(k % 2) * SEQ + (b + 1) * P],
                                        qa[:, b, k * P:(k + 1) * P], ident[:, :])
            last.then_inc(latent_trans, 1)
            wsl = take("C").rearrange("p (k n) -> p k n", k=KD)
            for c in range(4):
                feature_unit("cv", 4 + c, wsl, c, T0)
            pe.wait_ge(latentT_ready, 1)
            pe.wait_ge(dA_ready, 1)
            pe.wait_ge(consts_ready, 2)
            dAb = [dA[:, b * HEADS_S:(b + 1) * HEADS_S] for b in range(NB)]
            mm(bank[2][0:HEADS_S, 0:SEQ], dAb[0], metarows[:, :], True, False)
            mm(bank[2][0:HEADS_S, P:SEQ], dAb[2], tri[:, 0:P], False, False)
            mm(bank[2][0:HEADS_S, 0:SEQ], dAb[1], tri[:, :], False, True)
            for b, mats in enumerate([[trimeta], [metarows, tri], [metarows, ones, tri]]):
                for i, m in enumerate(mats):
                    last = mm(bank[3][:, b * HEADS_S:(b + 1) * HEADS_S], m[:, 0:P], dAb[i], i == 0, i == len(mats) - 1)
            last.then_inc(cum_done, 1)
            for half in range(2):
                wsl = take(f"uq{half}").rearrange("p (k n) -> p k n", k=KQ)
                for i in range(4 * half, 4 * half + 4):
                    b, part = i % 2, (i // 2) % 2
                    ps = unit("q", i)
                    for k in range(KQ):
                        last = mm(ps[:, 0:QL], qaT[:, k, b * P:(b + 1) * P], wsl[:, k, part * QL:(part + 1) * QL],
                                  k == 0, k == KQ - 1)
                    last.then_inc(proj_done, 1)
            ukv = take("ukv").rearrange("p (k n) -> p k n", k=KKV)
            for i in range(6):
                b, n = i // 2, i % 2
                ps = unit("v", i)
                for k in range(KKV):
                    last = mm(ps[:, :], ckvT[:, k, b * P:(b + 1) * P], ukv[:, k, 1024 + n * 512:1024 + (n + 1) * 512],
                              k == 0, k == KKV - 1)
                last.then_inc(proj_done, 1)

            def qk_head(h):
                if h >= 1:
                    pe.wait_ge(kT_ready, h)
                    pe.wait_ge(qT_ready, h)
                for k in range(KKV):
                    mm(bank[6][0:NOPE, 0:L], ukv[:, k, h * NOPE:(h + 1) * NOPE], ckvT[:, k, T0:T], k == 0, k == KKV - 1)
                for b in range(2):
                    last = pe.transpose(bank[7][0:QH, b * P:(b + 1) * P], q_sb[:, b, h * QH:(h + 1) * QH], ident[:, :])
                last.then_inc(qk_done, 1)

            def scores_head(h):
                pe.wait_ge(kT_ready, h + 1)
                pe.wait_ge(qT_ready, h + 1)
                if h >= 1:
                    pe.wait_ge(scores_read, h)
                mm(bank[2][:, 0:L - P], qTh[0:QH, h % 2, 0:P], kTh[0:QH, h % 2, 0:L - P])
                mm(bank[3][:, 0:L], qTh[0:QH, h % 2, P:SEQ], kTh[0:QH, h % 2, :]).then_inc(scores_done, 1)

            def probs_trans(h):
                pe.wait_ge(probs_ready, h + 1)
                if h >= 2 and h % 2 == 0:
                    pe.wait_ge(pv_read, h // 2)
                for b in range(2):
                    for qb in range(2):
                        pe.transpose(bank[4][:, b * SEQ + qb * P:b * SEQ + (qb + 1) * P],
                                     probs[:, h % 2, qb, b * P:(b + 1) * P], ident[:, :])
                pe.transpose(bank[5][:, 0:P], probs[:, h % 2, 1, 2 * P:T], ident[:, :]).then_inc(pT_done, 1)

            def pv_head(h):
                pe.wait_ge(pTa_ready, h + 1)
                pe.wait_ge(pTb_ready, h + 1)
                o = bank[5][(h % 2) * VH:(h % 2 + 1) * VH, P:3 * P]
                vh = [V[:, b, h * VH:(h + 1) * VH] for b in range(NB)]
                mm(o, vh[0], pT[:, 0:SEQ], True, False)
                mm(o[:, P:SEQ], vh[2], pT[:, 2 * SEQ:2 * SEQ + P], False, False)
                mm(o, vh[1], pT[:, SEQ:2 * SEQ], False, True).then_inc(pv_done, 1)

            pe.wait_ge(kpeT_ready, 2)
            pe.wait_ge(q_roped, 1)
            qk_head(0)
            pe.wait_ge(cum_read, 1)
            scores_head(0)
            for h in range(MH):
                if h + 1 < MH:
                    qk_head(h + 1)
                if h % 4 == 0:
                    wsl = take(f"xs{h // 4}").rearrange("p (k n) -> p k n", k=KD)
                feature_unit("cv", 8 + h, wsl, h % 4, T0)
                if h:
                    pv_head(h - 1)
                if h + 1 < MH:
                    scores_head(h + 1)
                probs_trans(h)
            pv_head(MH - 1)

            pe.wait_ge(pv_read, KD)
            for g in range(GROUPS):
                if g >= 2:
                    pe.wait_ge(cb_read, g - 1)
                ba, bb = bank[4 + 2 * (g % 2)], bank[5 + 2 * (g % 2)]
                mm(ba[:, 0:SEQ], BT[:, g, 0:P], CT[:, g, :])
                mm(ba[:, SEQ:2 * SEQ], BT[:, g, P:2 * P], CT[:, g, :])
                mm(bb[:, 0:P], BT[:, g, 2 * P:T], CT[:, g, P:SEQ]).then_inc(cb_done, 1)

            def acum_of(c):
                if c:
                    pe.wait_ge(diff_ready, c)
                for j in range(2):
                    last = mm(bank[2][:, j * SEQ:(j + 1) * SEQ], ident[:, 2 * c + j:2 * c + j + 1].to_broadcast([P, P]), AT[:, :])
                last.then_inc(acum_done, 1)

            def xtr_of(c):
                if c:
                    pe.wait_ge(xdt_ready, c)
                for b in range(NB):
                    last = pe.transpose(bank[6][:, b * P:(b + 1) * P], xT[:, c, b * P:(b + 1) * P], ident[:, :])
                last.then_inc(xtr_done, 1)

            def gsum_of(c):
                pe.wait_ge(ysq_ready, c + 1)
                if c and c % CHUNKS_PER_GROUP == 0:
                    pe.wait_ge(gsum_read, c // CHUNKS_PER_GROUP)
                mm(bank[7][:, 0:SEQ], ones[:, :], ysq[:, c % 2, :], c % CHUNKS_PER_GROUP == 0,
                   c % CHUNKS_PER_GROUP == CHUNKS_PER_GROUP - 1).then_inc(gsum_done, 1)

            acum_of(0)
            pe.wait_ge(cb_read, GROUPS)
            pe.wait_ge(conv_fin, 24)
            xtr_of(0)
            for c in range(NX):
                if c + 1 < NX:
                    acum_of(c + 1)
                    xtr_of(c + 1)
                if c % 4 == 0:
                    wsl = take(f"z{c // 4}").rearrange("p (k n) -> p k n", k=KD)
                feature_unit("z", c, wsl, c % 4, P)
                pe.wait_ge(sc_ready, c + 1)
                if c:
                    pe.wait_ge(ssdy_read, c)
                for b, at, lo in ((0, 0, 0), (2, 2 * SEQ, P), (1, SEQ, 0)):
                    for j in range(2):
                        last = mm(bank[3][j * VH:(j + 1) * VH, lo:SEQ], xdt[:, c % 2, b, j * VH:(j + 1) * VH],
                                  decay[:, c % 2, j, at:at + SEQ - lo], b == 0, b == 1)
                last.then_inc(ssdy_done, 1)
                if c:
                    gsum_of(c - 1)
            gsum_of(NX - 1)
            for c in range(16):
                if c % 4 == 0:
                    wsl = take(f"g{c // 4}").rearrange("p (k n) -> p k n", k=KD)
                feature_unit("g", c, wsl, c % 4, P)
            pe.wait_ge(ssdy_read, NX)
            for m in range(2 * KD):
                if m < KD:
                    if m % 4 == 0:
                        wsl = take(f"wo{m // 4}").rearrange("p (k n) -> p k n", k=KD)
                    kn, src, j = KD, attnT, m % 4
                else:
                    if m % 2 == 0:
                        wsl = take(f"so{(m - KD) // 2}").rearrange("p (k n) -> p k n", k=NX)
                    kn, src, j = NX, y2T, m % 2
                if m == KD:
                    pe.wait_ge(yn_ready, NX)
                if m >= 2:
                    pe.wait_ge(merged, m - 1)
                for k in range(kn):
                    last = mm(bank[2 + m % 2][:, 0:SEQ], wsl[:, k, j * P:(j + 1) * P], src[:, k, :], k == 0, k == kn - 1)
                last.then_inc(out_done, 1)
            pe.wait_ge(merged, 2 * KD)
            pe.wait_ge(gsum_read, GROUPS)
            wout = [take(f"wout{n}").rearrange("p (k n) -> p k n", k=KD) for n in range(2)]

            def wout_unit(b, n, ks):
                for k in ks:
                    last = mm(bank[4 + 2 * n + b][:, :], mT[:, k, b * P:(b + 1) * P], wout[n][:, k, :], k == 0, k == KD - 1)
                return last

            def xn_transposes(b, n):
                pe.wait_ge(xn_ready, 2 * b + n + 1)
                for k in range(4):
                    last = pe.transpose(bank[2 * b + n][:, k * P:(k + 1) * P],
                                        xn[:, b, (4 * n + k) * P:(4 * n + k + 1) * P], ident[:, :])
                last.then_inc(xn_trans, 1)

            def logits(b):
                pe.wait_ge(h1_ready, 2 * b + 1)
                pe.wait_ge(xnT_ready, 2 * (b + 1))
                for k in range(KD):
                    last = mm(bank[4 + b][:, 0:E], xnT[:, b, k, :], v("w_router", k * E, E), k == 0, k == KD - 1)
                last.then_inc(logits_done, 1)

            wout_unit(0, 0, range(KD)).then_inc(wout_done, 1)
            wout_unit(0, 1, range(KD)).then_inc(wout_done, 1)
            xn_transposes(0, 0)
            wout_unit(1, 0, range(KD)).then_inc(wout_done, 1)
            xn_transposes(0, 1)
            wout_unit(1, 1, range(0, 3))
            logits(0)
            wout_unit(1, 1, range(3, KD)).then_inc(wout_done, 1)
            xn_transposes(1, 0)
            xn_transposes(1, 1)
            logits(1)
            pe.wait_ge(mask_ready, 2)
            mm(bank[6][:, 0:E], tri[:, 0:P], mask[:, 0, :])
            mm(bank[6][:, E:2 * E], ones[:, :], mask[:, 0, :], True, False)
            mm(bank[6][:, E:2 * E], tri[:, 0:P], mask[:, 1, :], False, True)
            mm(bank[6][:, 2 * E:3 * E], ones[:, :], mask[:, 0, :], True, False)
            mm(bank[6][:, 2 * E:3 * E], ones[:, :], mask[:, 1, :], False, True).then_inc(pos_done, 1)
            pe.wait_ge(route_ready, 1)
            for b in range(2):
                last = pe.transpose(bank[5][:, b * P:(b + 1) * P], wpad[:, b, :], ident[:, :])
            last.then_inc(w_trans, 1)
            def gather(n):
                pe.wait_ge(hot_ready, n)
                for b in range(2):
                    for j in range(2):
                        last = mm(bank[7][j * SLOTS:(j + 1) * SLOTS, :], hot[:, b, :], xn[:, b, j * 512:(j + 1) * 512], b == 0, b == 1)
                last.then_inc(gather_done, 1)

            def gather_trans(n):
                pe.wait_ge(xg_ready, n)
                for j in range(4):
                    last = pe.transpose(bank[7][:, j * P:(j + 1) * P], xg[:, j * P:(j + 1) * P], ident[:, :])
                last.then_inc(xg_trans, 1)

            FIRST = 0
            pe.wait_ge(xn_scaled, 2)
            gather(1)
            pe.wait_ge(wT_ready, 1)
            pe.wait_ge(bias_in, 32)
            for b in range(2):
                for n in range(2):
                    mm(bank[2 * b + n][:, :], wTs[:, b * P:(b + 1) * P], b2all[:, n * 512:(n + 1) * 512], True, False)

            def scatter(stop):
                for b in range(2):
                    for n in range(2):
                        last = mm(bank[2 * b + n][:, :], scat[:, n, b * P:(b + 1) * P], ob[:, :], False, stop)
                    if stop:
                        last.then_inc(scattered, 1)

            def expert_round(r):
                if r is not FIRST:
                    gather(r * (E + 1) + 1)
                gather_trans(r * (E + 1) + 1)
                with pe.Fori(0, E) as e:
                    t, g = r * E + e, r * (E + 1) + e + 1
                    pe.wait_ge(xgT_ready, g)
                    pe.wait_ge(bsel_ready, g)
                    pe.wait_ge(actT_ready, t + 1)
                    pe.wait_ge(scat_ready, t + 1)
                    for i in range(2):
                        for j in range(2):
                            mm(bank[4 + i][j * SLOTS:(j + 1) * SLOTS, :], bsel[:, :],
                               b1all[:, j * 1024 + i * 512:j * 1024 + (i + 1) * 512], True, False)
                    for k in range(KD):
                        pe.wait_ge(w1_in[k], 16 * (t + 1))
                        for i in range(2):
                            for j in range(2):
                                last = mm(bank[4 + i][j * SLOTS:(j + 1) * SLOTS, :],
                                          xgT[:, k % 4, (k // 4) * SLOTS:(k // 4 + 1) * SLOTS],
                                          w1_sb[k][:, j * 1024 + i * 512:j * 1024 + (i + 1) * 512], False, k == KD - 1)
                        if k < KD - 1:
                            last.then_inc(chunk_used, 1)
                    last.then_inc(up_done, 1)
                    gather(g + 1)
                    pe.wait_ge(ob_ready, t + 1)
                    scatter(False)
                    gather_trans(g + 1)
                    pe.wait_ge(hotw_ready, t + 1)
                    pe.wait_ge(up_read, t + 1)
                    for b in range(2):
                        last = pe.transpose(bank[5][:, b * P:(b + 1) * P], hotw[:, b, :, :].rearrange("p i s -> p (i s)"), ident[:, :])
                    last.then_inc(scat_trans, 1)
                    pe.wait_ge(act_ready, t + 1)
                    for j in range(4):
                        last = pe.transpose(bank[4][:, j * P:(j + 1) * P], act[:, j * P:(j + 1) * P], ident[:, :])
                    last.then_inc(act_trans, 1)
                    pe.wait_ge(actT_ready, t + 2)
                    for k in range(KD):
                        if k % 2 == 0:
                            pe.wait_ge(w2_in[k // 2], 16 * (t + 1))
                        for j in range(2):
                            last = mm(bank[6][j * SLOTS:(j + 1) * SLOTS, :], actT[:, k % 4, (k // 4) * SLOTS:(k // 4 + 1) * SLOTS],
                                      w2_sb[k // 2][:, k % 2, j * 512:(j + 1) * 512], k == 0, k == KD - 1)
                        if k % 2 and k < KD - 1:
                            last.then_inc(chunk_used, 1)
                    last.then_inc(down_done, 1)

            expert_round(FIRST)
            pe.wait_ge(count_ready, 1)
            cm = pe.value_load(cmax_i[0:1, 0:1], min_val=0, max_val=SEQ)
            with pe.If(cm > SLOTS):
                with pe.Fori(1, SEQ // SLOTS) as r:
                    expert_round(r)
                pe.wait_ge(ob_ready, E * (SEQ // SLOTS) + 1)
                pe.wait_ge(scat_ready, E * (SEQ // SLOTS) + 1)
            pe.wait_ge(ob_ready, E + 1)
            pe.wait_ge(scat_ready, E + 1)
            scatter(True)


def pack_slabs(inp):
    import numpy as np
    w_in, w_ukv = inp["w_in"][0], inp["w_ukv"][0].reshape(KVL, MH, NOPE + VH)

    def rows(a):
        return a.reshape(-1, P, a.shape[1]).transpose(1, 0, 2).reshape(P, -1)

    parts = {"dkv": np.concatenate([w_in[:, DT0:DT0 + HEADS_S], w_in[:, KV0:KV0 + KVL + ROPE]], axis=1),
             "qa": w_in[:, QA0:QA0 + QL], "B": w_in[:, B0:B0 + 512], "C": w_in[:, C0:C0 + 512],
             "ukv": np.concatenate([w_ukv[:, :, :NOPE].reshape(KVL, -1), w_ukv[:, :, NOPE:].reshape(KVL, -1)], axis=1)}
    for i in range(2):
        parts[f"uq{i}"] = inp["w_uq"][0][:, 768 * i:768 * (i + 1)]
        parts[f"wo{i}"] = inp["w_o"][0][:, 512 * i:512 * (i + 1)]
        parts[f"wout{i}"] = inp["w_out"][0][:, 512 * i:512 * (i + 1)]
    for i in range(4):
        parts[f"xs{i}"] = w_in[:, XS0 + 512 * i:XS0 + 512 * (i + 1)]
        parts[f"z{i}"] = w_in[:, Z0 + 512 * i:Z0 + 512 * (i + 1)]
        parts[f"g{i}"] = w_in[:, G0 + 512 * i:G0 + 512 * (i + 1)]
        parts[f"so{i}"] = inp["w_ssd_out"][0][:, 256 * i:256 * (i + 1)]
    return np.concatenate([rows(parts[name]) for name, _ in SLABS], axis=1)


def pack_vectors(inp):
    import numpy as np

    def cols(a):
        return a.reshape(-1, P).T

    pos = np.arange(L, dtype=np.float32)
    inv = np.float32(10000.0) ** (-np.arange(0, ROPE, 2, dtype=np.float32) / np.float32(ROPE))
    ang = np.concatenate([np.zeros((T0, 16), np.float32), pos[:, None] * inv[None, :]])
    blocks = {
        "norm_mix": cols(inp["norm_mix"][0]),
        "conv_w": np.roll(inp["conv_w"][0].reshape(4, 24, P), 8, axis=1).transpose(2, 1, 0).reshape(P, -1),
        "conv_b": np.roll(cols(inp["conv_b"][0]), 8, axis=1), "ssd_norm": cols(inp["ssd_norm"][0]),
        "d_skip": cols(np.repeat(inp["d_skip"][0], 64)), "q_norm": cols(inp["q_norm"][0]),
        "kv_norm": cols(inp["kv_norm"][0]),
        "cos": np.cos(ang).reshape(NB, P, 16).transpose(1, 0, 2).reshape(P, -1),
        "sin": np.sin(ang).reshape(NB, P, 16).transpose(1, 0, 2).reshape(P, -1),
        "w_router": inp["w_router"][0].reshape(KD, P, E).transpose(1, 0, 2).reshape(P, -1),
    }
    for name in ("dt_bias", "a_log", "b_router"):
        blocks[name] = np.broadcast_to(inp[name][0][None, :], (P, E))
    return np.concatenate([blocks[name] for name in VEC], axis=1).astype(np.float32)


def kernel(**inputs):
    import numpy as np
    import concourse.bacc as bacc
    from concourse.bass_utils import run_bass_kernel_spmd

    inp = {k: np.asarray(a) for k, a in inputs.items()}
    arrays = {
        "x": inp["x"][0], "meta": inp["meta_tokens"], "slabs": pack_slabs(inp), "vecs": pack_vectors(inp),
        "rows": np.broadcast_to(np.concatenate([inp["norm_ffn"][0], inp["norm_final"]])[None, :], (P, 2 * D)),
        "w1": inp["w_mlp1"].reshape(E * D, 2 * DE), "b1": inp["b_mlp1"][0],
        "w2": inp["w_mlp2"].reshape(E * DE, D), "b2": inp["b_mlp2"][0],
    }
    arrays = {f"{k}_dram": np.ascontiguousarray(a) for k, a in arrays.items()}
    nc = bacc.Bacc("TRN2", target_bir_lowering=False, num_devices=1)
    args = [nc.dram_tensor(k, a.shape, mybir.dt.from_np(a.dtype), kind="ExternalInput").ap() for k, a in arrays.items()]
    out = nc.dram_tensor("out_dram", (SEQ, D), F32, kind="ExternalOutput").ap()
    meta_ssd_mla_moe(nc, *args, out)
    r = run_bass_kernel_spmd(nc, [arrays], core_ids=[0])
    return r.results[0]["out_dram"].reshape(1, SEQ, D)
```

```python
import concourse.bass as bass
from concourse import mybir
from contextlib import ExitStack

F32 = mybir.dt.float32
F32R = mybir.dt.float32r
I32 = mybir.dt.int32
U32 = mybir.dt.uint32
ALU = mybir.AluOpType
ACT = mybir.ActivationFunctionType
AX = mybir.AxisListType

P = 128
D = 1024
KD = D // P
NMETA, SEQ = 16, 256
NB = 3
T = NB * P
T0 = P - NMETA
L = NMETA + SEQ
DI = 2048
NX = DI // P
HEADS_S = 32
GROUPS = 4
CHUNKS_PER_GROUP = NX // GROUPS
MH = 16
NOPE, ROPE, VH = 64, 32, 64
QH = NOPE + ROPE
QL, KVL = 384, 256
KQ, KKV = QL // P, KVL // P
E = 32
TOPK = 4
DE = 1024
SLOTS = 64
EPS, MLA_EPS = 1e-5, 1e-6
ALPHA, LIMIT = 1.702, 7.0
NEG = -1.0e30

Z0, XS0, B0, C0 = 0, DI, 2 * DI, 2 * DI + GROUPS * P
DT0 = C0 + GROUPS * P
QA0 = DT0 + HEADS_S
KV0 = QA0 + QL
G0 = KV0 + KVL + ROPE
DKV = HEADS_S + KVL + ROPE

SLABS = [("dkv", KD * DKV), ("qa", KD * QL), ("B", KD * 512), ("C", KD * 512),
         ("uq0", KQ * 768), ("uq1", KQ * 768), ("ukv", KKV * 2048)]
SLABS += [(f"xs{i}", KD * 512) for i in range(4)] + [(f"z{i}", KD * 512) for i in range(4)]
SLABS += [(f"g{i}", KD * 512) for i in range(4)] + [(f"wo{i}", KD * 512) for i in range(2)]
SLABS += [(f"so{i}", NX * 256) for i in range(4)] + [(f"wout{i}", KD * 512) for i in range(2)]
SLAB = {name: i for i, (name, _) in enumerate(SLABS)}
SLOT_OF = {"dkv": 0, "qa": 1, "B": 2, "C": 0, "uq0": 1, "uq1": 2, "ukv": 0, "xs0": 1, "xs1": 2, "xs2": 1, "xs3": 2, "z0": 1}
SLOT_OF.update({name: (0, 2, 1)[i % 3] for i, (name, _) in enumerate(SLABS[SLAB["z1"]:])})
NEIGHBOURS = {s: [name for name, _ in SLABS if SLOT_OF[name] == s] for s in range(3)}
OFF = [sum(n for _, n in SLABS[:i]) for i in range(len(SLABS))]
SLAB_COLS = OFF[-1] + SLABS[-1][1]
NSLOT, SLOT = 6, 4096

PIECE = KD * P
NSPLIT = 3

W1_AT = [(3, 0), (3, 2048), (4, 0), (4, 2048), (5, 0), (5, 2048), (0, 0), (0, 2048)]
W2_AT = [(1, 0), (1, 2048), (2, 0), (2, 2048)]
CHUNKS = len(W1_AT) + len(W2_AT)
SIGNALS = CHUNKS - 2

VEC = {}
_at = 0
for _name, _n in [("norm_mix", KD), ("conv_w", 4 * 24), ("conv_b", 24), ("ssd_norm", NX), ("d_skip", NX),
                  ("q_norm", KQ), ("kv_norm", KKV), ("dt_bias", E), ("a_log", E), ("b_router", E),
                  ("cos", NB * 16), ("sin", NB * 16), ("w_router", KD * E)]:
    VEC[_name] = (_at, _at + _n)
    _at += _n
VEC_COLS = _at


WORK = 25736


def meta_ssd_mla_moe(nc, x, meta, slabs, vecs, rows, w1, b1, w2, b2, out):
    ctx = ExitStack()
    with ctx:
        def sb(name, cols, dt=F32):
            return ctx.enter_context(nc.sbuf_tensor(name, [P, cols], dt))

        IN_WORK = NSLOT * SLOT
        overlays, end = {}, 0
        with ExitStack() as lent:
            for name, at, n in [("hn_lo", 3 * SLOT, KD * T), ("AT_hi", 3 * SLOT + 3072, SEQ), ("AT_lo", 3 * SLOT + 3072 + SEQ, SEQ),
                                ("head_row", 3 * SLOT + 3072 + 2 * SEQ, HEADS_S), ("split0", 4 * SLOT, 2 * PIECE), ("split1", 4 * SLOT + 2 * PIECE, 2 * PIECE),
                                ("attn_lo", 5 * SLOT, KD * SEQ), ("split2", 5 * SLOT + 2048, 2 * PIECE), ("hn_hi", IN_WORK, KD * T),
                                ("attn_hi", IN_WORK + 11776, KD * SEQ), ("y2_lo", IN_WORK + 13824, NX * SEQ),
                                ("y2_hi0", IN_WORK + 17920, KD * SEQ), ("y2_hi1", IN_WORK + 22528, KD * SEQ)]:
                if at > end:
                    lent.enter_context(nc.sbuf_tensor(f"before_{name}", [P, at - end], F32))
                overlays[name] = lent.enter_context(nc.sbuf_tensor(name, [P, n], F32R))
                end = at + n
        ring = sb("ring", NSLOT * SLOT)
        work = sb("work", WORK)
        vec = sb("vec", VEC_COLS)
        ident = sb("ident", P)
        ones = sb("ones", P)
        metarows = sb("metarows", 2 * P)
        tri = sb("tri", 2 * P)
        trimeta = sb("trimeta", P)
        keymask = sb("keymask", L)
        iota_slot = sb("iota_slot", SLOTS)
        iota_e = sb("iota_e", E)
        small = sb("small", 804)
        idx = sb("idx", 16, U32)
        cmax_i = sb("cmax_i", 1, I32)
        bank = [ctx.enter_context(nc.psum_tensor(f"bank{i}", [P, 512], F32)) for i in range(8)]

        def w(at, n):
            return work[:, at:at + n]

        def sm(at, n):
            return small[:, at:at + n]

        def v(name, i=0, n=None):
            a, b = VEC[name]
            return vec[:, a + i:(b if n is None else a + i + n)]

        hn_hi = overlays["hn_hi"][:, :].rearrange("p (k t) -> p k t", k=KD)
        hn_lo = overlays["hn_lo"][:, :].rearrange("p (k t) -> p k t", k=KD)
        AT_hi, AT_lo, head_row = overlays["AT_hi"], overlays["AT_lo"], overlays["head_row"]
        hnT = w(3072, 3072).rearrange("p (k t) -> p k t", k=KD)
        xT = w(3072, 6144).rearrange("p (c t) -> p c t", c=NX)
        BT = w(9216, 1536).rearrange("p (g t) -> p g t", g=GROUPS)
        CT = w(10752, 1024).rearrange("p (g t) -> p g t", g=GROUPS)
        attn_hi = overlays["attn_hi"][:, :].rearrange("p (k t) -> p k t", k=KD)
        attn_lo = overlays["attn_lo"][:, :].rearrange("p (k t) -> p k t", k=KD)
        split = [overlays[f"split{i}"][:, :].rearrange("p (i k n) -> p i k n", i=2, k=KD) for i in range(NSPLIT)]
        R = 13824
        xtok = w(R, 3072).rearrange("p (b d) -> p b d", b=NB)
        q_sb = w(R, 3072).rearrange("p (b d) -> p b d", b=2)
        V = w(R + 3072, 3072).rearrange("p (b d) -> p b d", b=NB)
        mid = w(R + 3072, 960).rearrange("p (b d) -> p b d", b=NB)
        qa = w(R + 4032, 768).rearrange("p (b d) -> p b d", b=2)
        ckk = w(R + 4800, 1056).rearrange("p (b d) -> p b d", b=NB)
        ckvT = w(R + 6144, 768).rearrange("p (k t) -> p k t", k=KKV)
        qaT = w(R + 6912, 768).rearrange("p (k t) -> p k t", k=KQ)
        pT = w(R + 6912, 640)
        kTh = w(R + 7680, 544).rearrange("p (i t) -> p i t", i=2)
        qTh = w(R + 8224, 512).rearrange("p (i t) -> p i t", i=2)
        probs = w(R + 8736, 1536).rearrange("p (i b t) -> p i b t", i=2, b=2)
        xraw = w(R + 10272, 550).rearrange("p (i t) -> p i t", i=2)
        conv = w(R + 10822, 544).rearrange("p (i t) -> p i t", i=2)
        convt = w(R + 11366, 544).rearrange("p (i t) -> p i t", i=2)
        junk = w(6144, 3072).rearrange("p (b d) -> p b d", b=NB)
        junk2 = w(11776, 2048)
        ropet = w(3072, 2048).rearrange("p (i h r) -> p i h r", i=8, r=16)
        y2T = w(R, 4096).rearrange("p (c t) -> p c t", c=NX)
        CBm = w(R + 4096, 2560).rearrange("p (g t) -> p g t", g=GROUPS)
        decay = w(R + 6656, 2560).rearrange("p (i j t) -> p i j t", i=2, j=2)
        y2_lo = overlays["y2_lo"][:, :].rearrange("p (c t) -> p c t", c=NX)
        y2_hi = [overlays[f"y2_hi{i // 8}"][:, (i % 8) * SEQ:(i % 8 + 1) * SEQ] for i in range(NX)]
        xdt = w(R + 9216, 768).rearrange("p (i b t) -> p i b t", i=2, b=NB)
        ztanh = w(R + 9984, 512).rearrange("p (i t) -> p i t", i=2)
        zcopy = w(R + 10496, 512).rearrange("p (i t) -> p i t", i=2)
        ysq = w(R + 11008, 512).rearrange("p (i t) -> p i t", i=2)
        zw = w(9216, 256)
        yv = w(9472, 256)
        var_g = w(9728, GROUPS * 256)
        rstd_g, tmp_g = w(R + 6656, GROUPS * 256), w(R + 7680, GROUPS * 256)
        gt = w(3072, 4096).rearrange("p (c t) -> p c t", c=16)
        mT = w(7168, 2048).rearrange("p (k t) -> p k t", k=KD)
        mtmp = w(11264, 512).rearrange("p (i t) -> p i t", i=2)
        xres = w(9216, 2048).rearrange("p (b d) -> p b d", b=2)
        h1 = w(R, 2048).rearrange("p (b d) -> p b d", b=2)
        xn = w(R + 2048, 2048).rearrange("p (b d) -> p b d", b=2)
        xnT = w(R + 6656, 2048).rearrange("p (b k t) -> p b k t", b=2, k=KD)
        hsq = w(3072, 1024).rearrange("p (i d) -> p i d", i=2)
        chosen = w(R + 10752, 256).rearrange("p (b j e) -> p b j e", b=2, j=TOPK)
        nf = w(11776, 1024)
        nfin = w(12800, 1024)
        b1all = w(0, 2048)
        b2all = w(2048, 1024)
        xg = w(3072, 512)
        xgT = w(3584, 512).rearrange("p (j t) -> p j t", j=4)
        actT = w(4096, 512).rearrange("p (j t) -> p j t", j=4)
        glu = w(4608, 512)
        lin = w(5120, 512)
        sig = w(5632, 512)
        act = w(6144, 512)
        ob = w(6656, 512)
        scat = w(7168, 512).rearrange("p (n t) -> p n t", n=2)
        hot = w(7680, 128).rearrange("p (b s) -> p b s", b=2)
        hotw = w(7808, 256).rearrange("p (b i s) -> p b i s", b=2, i=2)
        bsel = w(8064, SLOTS)
        pw = w(8128, 4)
        wpad = w(5632, 256).rearrange("p (b t) -> p b t", b=2)
        fin = w(4096, 2048).rearrange("p (b d) -> p b d", b=2)

        ssx, ssk, ssq = sm(0, 3), sm(3, 3), sm(6, 2)
        rsx, rsk, rsq = sm(8, 3), sm(11, 3), sm(14, 2)
        dtv, dta, dt = sm(16, 96), sm(112, 96), sm(208, 96)
        dA, As = sm(304, 96), sm(400, 96)
        AT = sm(496, 256)
        negA = sm(752, 32)
        rmax, nmax = sm(784, 2), sm(786, 4).rearrange("p (i b) -> p i b", i=2)
        rsum = sm(790, 4).rearrange("p (i b) -> p i b", i=2)
        rinv = sm(794, 2)
        kr = w(R + 6912, 192).rearrange("p (i b r) -> p i b r", i=4, b=NB)
        wTs = sm(208, 256)
        lg = sm(16, 64).rearrange("p (b e) -> p b e", b=2)
        mx8 = sm(80, 16).rearrange("p (b e) -> p b e", b=2)
        idxf = sm(96, 16).rearrange("p (b e) -> p b e", b=2)
        e4 = sm(112, 8).rearrange("p (b e) -> p b e", b=2)
        nm4, s4, r4 = sm(120, 2), sm(122, 2), sm(124, 2)
        mask = sm(496, 64).rearrange("p (b e) -> p b e", b=2)
        rsn = sm(564, 2)
        ssh4 = sm(560, 4).rearrange("p (b n) -> p b n", b=2)
        PW = sm(624, 132).rearrange("p (i e) -> p i e", i=4)
        ssh, rsh, cmax = sm(796, 2), sm(798, 2), sm(800, 1)
        nrt = sm(801, 3)

        def sem(name):
            return ctx.enter_context(nc.semaphore(name))

        vec_in, x_in = sem("vec_in"), [sem(f"x_in{b}") for b in range(NB)]
        slab_in = [sem(f"slab_in{i}") for i in range(3)]
        hn_hi_ready, hn_lo_ready, hi_ready, lo_ready = sem("hn_hi_ready"), sem("hn_lo_ready"), sem("hi_ready"), sem("lo_ready")
        so_half, attn_hi_ready, y2_hi_ready, y2_lo_ready = sem("so_half"), sem("attn_hi_ready"), sem("y2_hi_ready"), sem("y2_lo_ready")
        xres_in, rows_in, bias_in = sem("xres_in"), sem("rows_in"), sem("bias_in")
        w1_in = [sem(f"w1_in{i}") for i in range(len(W1_AT))]
        w1_odd_in = [sem(f"w1_odd_in{i}") for i in range(5)]
        w2_in = [sem(f"w2_in{i}") for i in range(len(W2_AT))]
        chunk_used = sem("chunk_used")
        pool_step, dve_step, act_step = sem("pool_step"), sem("dve_step"), sem("act_step")
        consts_ready, zeros_ready, meta_zero = sem("consts_ready"), sem("zeros_ready"), sem("meta_zero")
        x_squared, hn_ready, hn_trans, hnT_ready = sem("x_squared"), sem("hn_ready"), sem("hn_trans"), sem("hnT_ready")
        proj_done, proj_read = sem("proj_done"), sem("proj_read")
        latent_ready, latent_trans, latentT_ready = sem("latent_ready"), sem("latent_trans"), sem("latentT_ready")
        kpeT_ready, dt_abs, dt_ln, dA_ready = sem("kpeT_ready"), sem("dt_abs"), sem("dt_ln"), sem("dA_ready")
        cum_done, cum_read = sem("cum_done"), sem("cum_read")
        conv_done, conv_tanh, conv_fin = sem("conv_done"), sem("conv_tanh"), sem("conv_fin")
        q_roped = sem("q_roped")
        qk_done, kT_ready, qT_ready = sem("qk_done"), sem("kT_ready"), sem("qT_ready")
        scores_done, scores_read, exp_done, probs_ready = sem("scores_done"), sem("scores_read"), sem("exp_done"), sem("probs_ready")
        pT_done, pTa_ready, pTb_ready = sem("pT_done"), sem("pTa_ready"), sem("pTb_ready")
        pv_done, pv_read = sem("pv_done"), sem("pv_read")
        cb_done, cb_read = sem("cb_done"), sem("cb_read")
        zw_ready = sem("zw_ready")
        diff2_ready, AT_hi_ready, AT_lo_ready = sem("diff2_ready"), sem("AT_hi_ready"), sem("AT_lo_ready")
        acum_done, diff_ready, decay_exp, sc_ready = sem("acum_done"), sem("diff_ready"), sem("decay_exp"), sem("sc_ready")
        xtr_done, xdt_ready = sem("xtr_done"), sem("xdt_ready")
        ssdy_done, ssdy_read, y2_ready, ysq_ready = sem("ssdy_done"), sem("ssdy_read"), sem("y2_ready"), sem("ysq_ready")
        gsum_done, gsum_read, yn_ready = sem("gsum_done"), sem("gsum_read"), sem("yn_ready")
        out_done, merged = sem("out_done"), sem("merged")
        wout_done, h1_ready, h1_squared, xn_ready = sem("wout_done"), sem("h1_ready"), sem("h1_squared"), sem("xn_ready")
        xn_trans, xnT_ready, xn_scaled = sem("xn_trans"), sem("xnT_ready"), sem("xn_scaled")
        rsn_ready, mask_ready, w_trans = sem("rsn_ready"), sem("mask_ready"), sem("w_trans")
        logits_done, top_ready, top_exp, route_ready = sem("logits_done"), sem("top_ready"), sem("top_exp"), sem("route_ready")
        pos_done, wT_ready, count_ready = sem("pos_done"), sem("wT_ready"), sem("count_ready")
        moe_zero, moe_step = sem("moe_zero"), sem("moe_step")
        hot_ready, hotw_ready, bsel_ready = sem("hot_ready"), sem("hotw_ready"), sem("bsel_ready")
        gather_done, xg_ready, xg_trans, xgT_ready = sem("gather_done"), sem("xg_ready"), sem("xg_trans"), sem("xgT_ready")
        up_done, glu_ready, up_read, sig_ready = sem("up_done"), sem("glu_ready"), sem("up_read"), sem("sig_ready")
        act_ready, scat_trans, scat_ready, act_trans, actT_ready = (sem("act_ready"), sem("scat_trans"), sem("scat_ready"),
                                                                   sem("act_trans"), sem("actT_ready"))
        down_done, ob_ready, scattered = sem("down_done"), sem("ob_ready"), sem("scattered")
        h2_ready, h2_squared, y_ready, y_out = sem("h2_ready"), sem("h2_squared"), sem("y_ready"), sem("y_out")

        ORDER = (1, 2, 0)
        UNITS = [("dkv", b) for b in ORDER] + [("qa", b) for b in (1, 2)]
        UNITS += [("cv", c) for c in range(8)] + [("q", i) for i in range(8)] + [("v", i) for i in range(6)]
        UNITS += [("cv", 8 + c) for c in range(NX)] + [("z", c) for c in range(NX)] + [("g", c) for c in range(16)]
        U = {key: u for u, key in enumerate(UNITS)}

        def slab(name):
            at = SLOT_OF[name] * SLOT
            return ring[:, at:at + SLABS[SLAB[name]][1]]

        def arrived(name):
            s = SLOT_OF[name]
            return slab_in[s], 16 * (NEIGHBOURS[s].index(name) + 1)

        PIECES = [(("B", "C", "xs0", "xs1", "xs2", "xs3")[c // 4], c % 4, (proj_done, U["cv", c] + 1)) for c in range(24)]
        PIECES += [(f"z{c // 4}", c % 4, (proj_done, U["z", c] + 1)) for c in range(NX)]
        PIECES += [(f"g{c // 4}", c % 4, (proj_done, U["g", c] + 1)) for c in range(16)]
        PIECES += [(f"wo{m // 4}", m % 4, (out_done, m + 1)) for m in range(KD)]
        PIECES += [(f"so{m // 2}", 2 * (m % 2) + h, (out_done, KD + m + 1) if h else (so_half, m + 1)) for m in range(KD) for h in range(2)]
        PZ, PG = 24, 24 + NX
        PWO = PG + 16
        PSO = PWO + KD

        def piece(p):
            name, part, _ = PIECES[p]
            if p < PSO:
                return slab(name).rearrange("p (k n) -> p k n", k=KD)[:, :, part * P:(part + 1) * P]
            j, h = part // 2, part % 2
            return slab(name).rearrange("p (k n) -> p k n", k=NX)[:, h * KD:(h + 1) * KD, j * P:(j + 1) * P]

        w1_sb = [ring[:, s * SLOT + o:s * SLOT + o + 2048] for s, o in W1_AT]
        w1_odd = [w(at, 2048) for at in (R + 4096, R + 8704, R + 6656, 8704, 10752)]
        w2_sb = [ring[:, s * SLOT + o:s * SLOT + o + 2048].rearrange("p (j n) -> p j n", j=2) for s, o in W2_AT]
        used = {"dkv": (proj_done, U["dkv", ORDER[-1]] + 1), "qa": (proj_done, U["qa", 2] + 1), "uq0": (proj_done, U["q", 3] + 1),
                "uq1": (proj_done, U["q", 7] + 1), "ukv": (qk_done, MH), "wout0": (wout_done, 3), "wout1": (wout_done, 4)}
        for p, (name, _, _) in enumerate(PIECES):
            used[name] = (lo_ready, p + 1)

        DECAY_AT = [(0, 0), (0, SEQ), (P, 2 * SEQ)]

        def norm_stage(u):
            n = 2 * (u // 3) + u % 3
            return (None, None) if u % 3 == 2 else (n // 4, n % 4)

        block = ctx.enter_context(nc.Block())

        @block.sync
        def _(sp):
            sp.dma_start(xtok[:, 1, :], x[0:P, :]).then_inc(x_in[1], 16)
            sp.dma_start(xtok[:, 2, :], x[P:2 * P, :]).then_inc(x_in[2], 16)
            sp.dma_start(vec[:, :], vecs).then_inc(vec_in, 16)
            sp.wait_ge(meta_zero, 1)
            sp.dma_start(xtok[T0:P, 0, :], meta).then_inc(x_in[0], 16)

            def first_expert(s, free):
                sp.wait_ge(*free)
                for k, (ks, _) in enumerate(W1_AT):
                    if ks == s:
                        sp.dma_start(w1_sb[k], w1[k * P:(k + 1) * P, :]).then_inc(w1_in[k], 16)
                for j, (js, _) in enumerate(W2_AT):
                    if js == s:
                        sp.dma_start(w2_sb[j], w2[2 * j * P:2 * (j + 1) * P, :].rearrange("(j p) n -> p j n", j=2)).then_inc(w2_in[j], 16)

            for i, (name, n) in enumerate(SLABS):
                s = SLOT_OF[name]
                turn = NEIGHBOURS[s].index(name)
                if turn:
                    sp.wait_ge(*used[NEIGHBOURS[s][turn - 1]])
                sp.dma_start(slab(name), slabs[:, OFF[i]:OFF[i] + n]).then_inc(slab_in[s], 16)
                if name == "so2":
                    first_expert(3, (proj_done, len(UNITS)))

            TURN = 11

            def load_w1(e, k, odd):
                buf, arrival = (w1_odd, w1_odd_in) if odd and k < len(w1_odd) else (w1_sb, w1_in)
                sp.dma_start(buf[k], w1[bass.ds(e * D + k * P, P), :]).then_inc(arrival[k], 16)

            def load_doubled(e, t, odd):
                for k in range(len(w1_odd)):
                    sp.wait_ge(chunk_used, (t - 2) * SIGNALS + k + 1)
                    load_w1(e, k, odd)

            def load_single(e, t):
                for k in range(len(w1_odd), len(W1_AT)):
                    if k < len(W1_AT) - 1:
                        sp.wait_ge(chunk_used, (t - 1) * SIGNALS + k + 1)
                    else:
                        sp.wait_ge(up_done, t)
                    load_w1(e, k, False)
                for j in range(len(W2_AT)):
                    if j < len(W2_AT) - 1:
                        sp.wait_ge(chunk_used, (t - 1) * SIGNALS + len(W1_AT) + j)
                    else:
                        sp.wait_ge(down_done, t)
                    sp.dma_start(w2_sb[j], w2[bass.ds(e * DE + 2 * j * P, 2 * P), :].rearrange("(j p) n -> p j n", j=2)).then_inc(w2_in[j], 16)

            def load_pairs(t0, first):
                with sp.Fori(first, E // 2) as i:
                    for odd in (0, 1):
                        load_doubled(2 * i + odd, t0 + 2 * i + odd, odd)
                        load_single(2 * i + odd, t0 + 2 * i + odd)

            first_expert(0, used[NEIGHBOURS[0][-1]])
            first_expert(4, (out_done, 2 * KD))
            first_expert(5, (out_done, 2 * KD))
            load_w1(1, 0, True)
            load_w1(1, 1, True)
            for s in (2, 1):
                first_expert(s, used[NEIGHBOURS[s][-1]])
            sp.wait_ge(xn_ready, 4)
            load_w1(1, 3, True)
            load_w1(1, 4, True)
            sp.wait_ge(logits_done, 2)
            load_w1(1, 2, True)
            load_doubled(2, 2, 0)
            load_single(1, 1)
            with sp.Fori(1, TURN) as i:
                for odd in (0, 1):
                    e = 2 * i + odd
                    load_doubled(e + 1, e + 1, 1 - odd)
                    load_single(e, e)
            load_single(2 * TURN, 2 * TURN)
            load_doubled(2 * TURN + 1, 2 * TURN + 1, 1)
            load_single(2 * TURN + 1, 2 * TURN + 1)
            load_pairs(0, TURN + 1)
            sp.wait_ge(count_ready, 1)
            cm = sp.value_load(cmax_i[0:1, 0:1], min_val=0, max_val=SEQ)
            with sp.If(cm > SLOTS):
                with sp.Fori(1, SEQ // SLOTS) as r:
                    load_pairs(r * E, 0)
            for b in range(2):
                sp.wait_ge(y_ready, b + 1)
                sp.dma_start(out[b * P:(b + 1) * P, :], fin[:, b, :]).then_inc(y_out, 16)
            sp.wait_ge(y_out, 32)

        @block.gpsimd
        def _(pool):
            steps = 0

            def link(ins):
                nonlocal steps
                steps += 1
                ins.then_inc(pool_step, 1)
                pool.wait_ge(pool_step, steps)

            pool.memset(xtok[:, 0, :], 0.0).then_inc(meta_zero, 1)
            link(pool.memset(ident[:, :], 0.0))
            pool.affine_select(out=ident[:, :], in_=ident[:, :], pattern=[[-1, P]], compare_op=ALU.not_equal, fill=1.0,
                               base=0, channel_multiplier=1).then_inc(consts_ready, 1)
            pool.memset(xraw[:, :, 0:3], 0.0).then_inc(zeros_ready, 1)
            link(pool.memset(ones[:, :], 1.0))
            link(pool.memset(tri[:, :], 1.0))
            link(pool.affine_select(out=tri[:, 0:P], in_=tri[:, 0:P], pattern=[[1, P]], compare_op=ALU.is_ge, fill=0.0,
                                    base=0, channel_multiplier=-1))
            link(pool.memset(metarows[:, :], 1.0))
            link(pool.affine_select(out=metarows[:, :], in_=metarows[:, :], pattern=[[0, 2 * P]], compare_op=ALU.is_ge,
                                    fill=0.0, base=-T0, channel_multiplier=1))
            link(pool.affine_select(out=trimeta[:, :], in_=tri[:, 0:P], pattern=[[0, P]], compare_op=ALU.is_ge,
                                    fill=0.0, base=-T0, channel_multiplier=1))
            link(pool.memset(keymask[:, :], 0.0))
            link(pool.affine_select(out=keymask[:, L - P:L], in_=keymask[:, L - P:L], pattern=[[-1, P]],
                                    compare_op=ALU.is_ge, fill=NEG, base=0, channel_multiplier=1))
            link(pool.iota(iota_slot[:, :], pattern=[[1, SLOTS]], base=0, channel_multiplier=0,
                           allow_small_or_imprecise_dtypes=True))
            link(pool.iota(iota_e[:, :], pattern=[[1, E]], base=0, channel_multiplier=0,
                           allow_small_or_imprecise_dtypes=True))
            link(pool.memset(AT[:, :], 0.0))
            link(pool.memset(probs[:, :, :, 0:T0], 0.0))
            pool.memset(BT[:, :, 0:T0], 0.0).then_inc(consts_ready, 1)
            pool.wait_ge(q_roped, 1)
            pool.memset(xT[:, :, 0:T0], 0.0).then_inc(zeros_ready, 1)
            for c in range(NX):
                pool.wait_ge(proj_read, U["z", c] + 1)
                link(pool.tensor_scalar(ztanh[:, c % 2, :], ztanh[:, c % 2, :], 1.0, None, ALU.add))
                if c:
                    pool.wait_ge(y2_ready, c)
                pool.tensor_tensor(zw, ztanh[:, c % 2, :], zcopy[:, c % 2, :], ALU.mult).then_inc(zw_ready, 1)
            pool.wait_ge(diff_ready, NX)
            pool.wait_ge(diff2_ready, NX)
            pool.memset(PW[:, :, :], -1.0).then_inc(moe_zero, 1)
            for c in range(NX):
                pool.wait_ge(y2_hi_ready, c + 1)
                pool.tensor_tensor(y2_lo[:, c, :], y2T[:, c, :], y2_hi[c], ALU.subtract).then_inc(y2_lo_ready, 1)
            pool.wait_ge(proj_done, len(UNITS))
            pool.memset(w(0, 3072), 0.0).then_inc(moe_zero, 1)
            pool.wait_ge(moe_zero, 2)
            pool.dma_start(b1all[0:E, :], b1).then_inc(bias_in, 16)
            pool.dma_start(b2all[0:E, :], b2).then_inc(bias_in, 16)
            pool.wait_ge(yn_ready, NX)
            pool.dma_start(xres[:, 0, :], x[0:P, :]).then_inc(xres_in, 16)
            pool.dma_start(xres[:, 1, :], x[P:2 * P, :]).then_inc(xres_in, 16)
            pool.wait_ge(out_done, KD)
            pool.dma_start(w(11776, 2048), rows).then_inc(rows_in, 16)
            pool.wait_ge(merged, 2 * KD)
            pool.memset(wpad[:, :, :], 0.0).then_inc(moe_zero, 1)
            pool.memset(ob[:, :], 0.0).then_inc(ob_ready, 1)
            pool.memset(actT[:, :, :], 0.0).then_inc(actT_ready, 1)
            for b in range(2):
                if b == 1:
                    pool.wait_ge(wout_done, 4)
                    pool.memset(scat[:, :, :], 0.0).then_inc(scat_ready, 1)
                pool.wait_ge(rsn_ready, b + 1)
                pool.wait_ge(xn_trans, 2 * (b + 1))
                pool.tensor_scalar(xn[:, b, :], xn[:, b, :], rsn[:, b:b + 1], None, ALU.mult).then_inc(xn_scaled, 1)

        @block.scalar
        def _(a):
            for b in ORDER:
                a.wait_ge(x_in[b], 16)
                a.activation(junk[:, b, :], xtok[:, b, :], ACT.Square, accum_out=ssx[:, b:b + 1]).then_inc(x_squared, 1)

            def unit(kind, i):
                u = U[kind, i]
                a.wait_ge(proj_done, u + 1)
                return bank[u % 2]

            for i in range(6):
                b, k = ORDER[i // 2], 4 * (i % 2)
                a.wait_ge(hnT_ready, i + 1)
                a.activation(hn_hi[:, k:k + 4, b * P:(b + 1) * P], hnT[:, k:k + 4, b * P:(b + 1) * P],
                             ACT.Copy).then_inc(hn_hi_ready, 1)

            def hi_of(p):
                a.wait_ge(*arrived(PIECES[p][0]))
                if p >= NSPLIT:
                    a.wait_ge(*PIECES[p - NSPLIT][2])
                a.activation(split[p % NSPLIT][:, 0], piece(p), ACT.Copy).then_inc(hi_ready, 1)

            for b in ORDER:
                ps = unit("dkv", b)
                a.activation(junk2[:, b * KVL:(b + 1) * KVL], ps[:, HEADS_S:HEADS_S + KVL], ACT.Square, accum_out=ssk[:, b:b + 1])
                a.activation(mid[:, b, :], ps[:, 0:DKV], ACT.Copy).then_inc(proj_read, 1)
            for p in range(NSPLIT):
                hi_of(p)
            for b in range(2):
                ps = unit("qa", b + 1)
                a.activation(junk2[:, 768 + b * QL:768 + (b + 1) * QL], ps[:, 0:QL], ACT.Square, accum_out=ssq[:, b:b + 1])
                a.activation(qa[:, b, :], ps[:, 0:QL], ACT.Copy).then_inc(proj_read, 1)

            def conv_in(c):
                ps = unit("cv", c)
                if c == 0:
                    a.wait_ge(zeros_ready, 1)
                if c >= 2:
                    a.wait_ge(conv_done, c - 1)
                a.activation(xraw[:, c % 2, 3:3 + L], ps[:, 0:L], ACT.Copy).then_inc(proj_read, 1)

            def tanh_of(c):
                a.wait_ge(conv_done, c + 1)
                if c >= 2:
                    a.wait_ge(conv_fin, c - 1)
                a.activation(convt[:, c % 2, :], conv[:, c % 2, :], ACT.Tanh).then_inc(conv_tanh, 1)

            for c in range(4):
                conv_in(c)
                hi_of(c + 3)
                if c:
                    tanh_of(c - 1)
            tanh_of(3)
            a.wait_ge(dt_abs, 1)
            a.activation(dt[:, :], dta[:, :], ACT.Exp, scale=-1.0).then_inc(act_step, 1)
            a.activation(negA[:, :], v("a_log"), ACT.Exp).then_inc(act_step, 1)
            a.wait_ge(act_step, 2)
            a.activation(dta[:, :], dt[:, :], ACT.Ln, bias=1.0).then_inc(dt_ln, 1)
            a.wait_ge(latent_trans, 1)
            for i in range(2):
                a.activation(kTh[NOPE:QH, i, :], bank[7][NOPE:QH, T0:T], ACT.Copy).then_inc(kpeT_ready, 1)
            for c in range(4, 8):
                conv_in(c)
                if c + 3 < 8:
                    hi_of(c + 3)
                if c > 4:
                    tanh_of(c - 1)
            tanh_of(7)
            for i in range(8):
                ps = unit("q", i)
                b, part = i % 2, i // 2
                a.activation(q_sb[:, b, part * QL:(part + 1) * QL], ps[:, 0:QL], ACT.Copy,
                             scale=float(QH) ** -0.5).then_inc(proj_read, 1)
            a.wait_ge(cum_read, 1)
            a.activation(head_row[:, :], ident[:, 0:HEADS_S], ACT.Copy)
            a.activation(AT_hi[:, :], AT[:, :], ACT.Copy).then_inc(AT_hi_ready, 1)
            a.wait_ge(dA_ready, 1)
            for i in range(6):
                ps = unit("v", i)
                a.activation(V[:, i // 2, (i % 2) * 512:(i % 2 + 1) * 512], ps[:, :], ACT.Copy).then_inc(proj_read, 1)
                if i in (2, 4):
                    hi_of(8 + i // 2 - 1)

            def k_head(h):
                a.wait_ge(qk_done, h + 1)
                a.activation(kTh[0:NOPE, h % 2, :], bank[6][0:NOPE, 0:L], ACT.Copy).then_inc(kT_ready, 1)

            def exp_head(h):
                a.wait_ge(scores_read, h + 1)
                a.activation(probs[:, h % 2, 0, T0:2 * P], probs[:, h % 2, 0, T0:2 * P], ACT.Exp,
                             bias=nmax[:, h % 2, 0:1], accum_out=rsum[:, h % 2, 0:1])
                a.activation(probs[:, h % 2, 1, T0:T], probs[:, h % 2, 1, T0:T], ACT.Exp,
                             bias=nmax[:, h % 2, 1:2], accum_out=rsum[:, h % 2, 1:2]).then_inc(exp_done, 1)

            k_head(0)
            exp_head(0)
            for h in range(MH):
                if h + 1 < MH:
                    k_head(h + 1)
                hi_of(8 + h + 2)
                conv_in(8 + h)
                if h:
                    tanh_of(8 + h - 1)
                if h and h % 2 == 0:
                    a.wait_ge(pv_done, h)
                    a.activation(attn_hi[:, h // 2 - 1, :], bank[3][:, 0:SEQ], ACT.Copy).then_inc(attn_hi_ready, 1)
                if h + 1 < MH:
                    exp_head(h + 1)
                a.wait_ge(pT_done, h + 1)
                a.activation(pT[:, 0:512], bank[4][:, :], ACT.Copy).then_inc(pTa_ready, 1)
            tanh_of(8 + MH - 1)
            a.wait_ge(pv_done, MH)
            a.activation(attn_hi[:, KD - 1, :], bank[3][:, 0:SEQ], ACT.Copy).then_inc(attn_hi_ready, 1)

            def diff2_of(c):
                a.wait_ge(acum_done, c + 1)
                if c == 0:
                    a.wait_ge(cb_read, GROUPS)
                if c >= 2:
                    a.wait_ge(ssdy_done, c - 1)
                for b, (lo, at) in enumerate(DECAY_AT):
                    col = b * HEADS_S + 2 * c + 1
                    last = a.activation(decay[:, c % 2, 1, at:at + SEQ - lo], bank[4][:, lo:SEQ], ACT.Relu,
                                        scale=-1.0, bias=As[:, col:col + 1])
                last.then_inc(diff2_ready, 1)

            def exp_decay(c):
                a.wait_ge(diff_ready, c + 1)
                a.activation(decay[:, c % 2, 0, :], decay[:, c % 2, 0, :], ACT.Exp)
                a.wait_ge(diff2_ready, c + 1)
                a.activation(decay[:, c % 2, 1, :], decay[:, c % 2, 1, :], ACT.Exp, scale=-1.0).then_inc(decay_exp, 1)

            def squares_of(c):
                a.wait_ge(y2_ready, c + 1)
                if c >= 2:
                    a.wait_ge(gsum_done, c - 1)
                a.activation(ysq[:, c % 2, :], y2T[:, c, :], ACT.Square, scale=0.5).then_inc(ysq_ready, 1)

            diff2_of(0)
            hi_of(PZ + 2)
            exp_decay(0)
            for c in range(NX):
                if c + 1 < NX:
                    diff2_of(c + 1)
                if c:
                    squares_of(c - 1)
                ps = unit("z", c)
                if c >= 2:
                    a.wait_ge(y2_ready, c - 1)
                a.activation(ztanh[:, c % 2, :], ps[:, 0:SEQ], ACT.Tanh, scale=0.5)
                a.activation(zcopy[:, c % 2, :], ps[:, 0:SEQ], ACT.Copy).then_inc(proj_read, 1)
                if c + 1 < NX:
                    exp_decay(c + 1)
                hi_of(PZ + c + 3)
            squares_of(NX - 1)
            for u in range(PSO - PG):
                if u:
                    hi_of(PG + u + 2)
                g, stage = norm_stage(u)
                if stage == 3:
                    a.wait_ge(yn_ready, CHUNKS_PER_GROUP * (g + 1))
                    for c in range(CHUNKS_PER_GROUP * g, CHUNKS_PER_GROUP * (g + 1)):
                        a.activation(y2_hi[c], y2T[:, c, :], ACT.Copy).then_inc(y2_hi_ready, 1)
                if u < 16:
                    ps = unit("g", u)
                    a.activation(gt[:, u, :], ps[:, 0:SEQ], ACT.Tanh, scale=0.5).then_inc(proj_read, 1)
            for p in range(PSO + 2, len(PIECES)):
                hi_of(p)
            def square_half(b, n):
                a.wait_ge(h1_ready, 2 * b + n + 1)
                if b:
                    a.wait_ge(h1_squared, 2 * b + n - 1)
                a.activation(hsq[:, n, :], h1[:, b, n * 512:(n + 1) * 512], ACT.Square,
                             accum_out=ssh4[:, b, n:n + 1]).then_inc(h1_squared, 1)

            def xn_copy(b, n):
                a.wait_ge(xn_trans, 2 * b + n + 1)
                a.activation(xnT[:, b, 4 * n:4 * n + 4, :].rearrange("p k t -> p (k t)"), bank[2 * b + n][:, :],
                             ACT.Copy).then_inc(xnT_ready, 1)

            def top_weights(b):
                a.wait_ge(top_ready, b + 1)
                a.activation(e4[:, b, :], mx8[:, b, 0:TOPK], ACT.Exp, bias=nm4[:, b:b + 1],
                             accum_out=s4[:, b:b + 1]).then_inc(top_exp, 1)

            square_half(0, 0)
            square_half(0, 1)
            xn_copy(0, 0)
            square_half(1, 0)
            xn_copy(0, 1)
            top_weights(0)
            square_half(1, 1)
            xn_copy(1, 0)
            xn_copy(1, 1)
            top_weights(1)
            a.wait_ge(w_trans, 1)
            a.activation(wTs[:, :], bank[5][:, 0:SEQ], ACT.Copy).then_inc(wT_ready, 1)

            def gathered(n):
                a.wait_ge(gather_done, n)
                a.activation(xg[:, :], bank[7][:, :], ACT.Copy).then_inc(xg_ready, 1)

            def gatheredT(n):
                a.wait_ge(xg_trans, n)
                a.activation(xgT[:, :, :].rearrange("p j t -> p (j t)"), bank[7][:, :], ACT.Copy).then_inc(xgT_ready, 1)

            def expert_round(r):
                gathered(r * (E + 1) + 1)
                gatheredT(r * (E + 1) + 1)
                with a.Fori(0, E) as e:
                    t, g = r * E + e, r * (E + 1) + e + 2
                    a.wait_ge(glu_ready, t + 1)
                    a.activation(sig[:, :], glu[:, :], ACT.Tanh, scale=0.5 * ALPHA).then_inc(sig_ready, 1)
                    gathered(g)
                    gatheredT(g)
                    a.wait_ge(act_trans, t + 1)
                    a.activation(actT[:, :, :].rearrange("p j t -> p (j t)"), bank[4][:, :], ACT.Copy,
                                 scale=0.5).then_inc(actT_ready, 1)
                    a.wait_ge(down_done, t + 1)
                    a.activation(ob[:, :], bank[6][:, :], ACT.Copy).then_inc(ob_ready, 1)

            expert_round(0)
            a.wait_ge(count_ready, 1)
            cm = a.value_load(cmax_i[0:1, 0:1], min_val=0, max_val=SEQ)
            with a.If(cm > SLOTS):
                with a.Fori(1, SEQ // SLOTS) as r:
                    expert_round(r)
            for b in range(2):
                a.wait_ge(h2_ready, b + 1)
                a.activation(w((3072, 9216)[b], 1024), h1[:, b, :], ACT.Square, accum_out=ssh[:, b:b + 1]).then_inc(h2_squared, 1)

        @block.vector
        def _(d):
            steps = 0

            def link(ins):
                nonlocal steps
                steps += 1
                ins.then_inc(dve_step, 1)
                d.wait_ge(dve_step, steps)

            def rsqrt_guess(y, val):
                yi = y.bitcast(I32)
                link(d.tensor_scalar(yi, val.bitcast(I32), 1, None, ALU.logical_shift_right))
                link(d.tensor_scalar(yi, yi, -1.0, 1597463007.0, ALU.mult, ALU.add))

            def newton(y, val, tmp):
                link(d.tensor_tensor(tmp, y, y, ALU.mult))
                link(d.scalar_tensor_tensor(tmp, val, -0.5, tmp, ALU.mult, ALU.mult))
                link(d.scalar_tensor_tensor(y, tmp, 1.5, y, ALU.add, ALU.mult))

            def rsqrt(y, val, tmp):
                rsqrt_guess(y, val)
                for _ in range(3):
                    newton(y, val, tmp)

            def rstd(dst, src, n, eps):
                cols = src.shape[1]
                link(d.tensor_scalar(src, src, 1.0 / n, eps, ALU.mult, ALU.add))
                rsqrt(dst, src, nrt[:, 0:cols])


            for i, b in enumerate(ORDER):
                d.wait_ge(x_squared, i + 1)
                rstd(rsx[:, b:b + 1], ssx[:, b:b + 1], D, EPS)
                d.tensor_scalar(xtok[:, b, :], xtok[:, b, :], rsx[:, b:b + 1], None, ALU.mult).then_inc(hn_ready, 1)
            d.wait_ge(vec_in, 16)
            for i in range(6):
                b, k = ORDER[i // 2], 4 * (i % 2)
                d.wait_ge(hn_trans, i + 1)
                d.tensor_tensor(hnT[:, k:k + 4, b * P:(b + 1) * P], bank[i][:, :].rearrange("p (k t) -> p k t", k=4),
                                v("norm_mix", k, 4).unsqueeze(2).to_broadcast([P, 4, P]), ALU.mult).then_inc(hnT_ready, 1)
            link(d.tensor_scalar(v("conv_w"), v("conv_w"), 0.5, None, ALU.mult))
            link(d.tensor_scalar(v("conv_b"), v("conv_b"), 0.5, None, ALU.mult))
            link(d.tensor_scalar(v("ssd_norm"), v("ssd_norm"), 0.5, None, ALU.mult))
            for i in range(6):
                b, k = ORDER[i // 2], 4 * (i % 2)
                d.wait_ge(hn_hi_ready, i + 1)
                at = (slice(None), slice(k, k + 4), slice(b * P, (b + 1) * P))
                d.tensor_tensor(hn_lo[at], hnT[at], hn_hi[at], ALU.subtract).then_inc(hn_lo_ready, 1)

            def lo_of(p):
                d.wait_ge(hi_ready, p + 1)
                d.tensor_tensor(split[p % NSPLIT][:, 1], piece(p), split[p % NSPLIT][:, 0], ALU.subtract).then_inc(lo_ready, 1)

            d.wait_ge(proj_read, 3)
            rstd(rsk, ssk, KVL, MLA_EPS)
            for b in range(NB):
                d.tensor_scalar(ckk[:, b, 0:KVL], mid[:, b, HEADS_S:HEADS_S + KVL], rsk[:, b:b + 1], None, ALU.mult)
            d.memset(ckk[:, :, KVL:KVL + NOPE], 0.0)
            k1, k2 = mid[:, :, HEADS_S + KVL:HEADS_S + KVL + 16], mid[:, :, HEADS_S + KVL + 16:DKV]
            cosv = v("cos").rearrange("p (b r) -> p b r", b=NB)
            sinv = v("sin").rearrange("p (b r) -> p b r", b=NB)
            d.tensor_tensor(kr[:, 0], k1, cosv, ALU.mult)
            d.tensor_tensor(kr[:, 1], k2, sinv, ALU.mult)
            d.tensor_tensor(kr[:, 2], k2, cosv, ALU.mult)
            link(d.tensor_tensor(kr[:, 3], k1, sinv, ALU.mult))
            d.tensor_tensor(ckk[:, :, KVL + NOPE:KVL + NOPE + 16], kr[:, 0], kr[:, 1], ALU.subtract)
            d.tensor_tensor(ckk[:, :, KVL + NOPE + 16:KVL + QH], kr[:, 2], kr[:, 3], ALU.add)
            dt3 = dtv.rearrange("p (b h) -> p b h", b=NB)
            link(d.tensor_tensor(dt3, mid[:, :, 0:HEADS_S], v("dt_bias").unsqueeze(1).to_broadcast([P, NB, HEADS_S]), ALU.add))
            d.scalar_tensor_tensor(dta[:, :], dtv[:, :], -1.0, dtv[:, :], ALU.mult, ALU.max).then_inc(dt_abs, 1)
            for p in range(NSPLIT):
                lo_of(p)
            d.wait_ge(proj_read, 5)
            rstd(rsq, ssq, QL, MLA_EPS)
            for b in range(2):
                last = d.tensor_scalar(qa[:, b, :], qa[:, b, :], rsq[:, b:b + 1], None, ALU.mult)
            last.then_inc(latent_ready, 1)

            def conv_of(c):
                d.wait_ge(proj_read, U["cv", c] + 1)
                if c >= 2:
                    d.wait_ge(conv_fin, c - 1)
                dst, src = conv[:, c % 2, :], xraw[:, c % 2, :]
                link(d.tensor_scalar(dst, src[:, 3:3 + L], v("conv_w", 4 * c + 3, 1), v("conv_b", c, 1), ALU.mult, ALU.add))
                for j in (0, 1):
                    link(d.scalar_tensor_tensor(dst, src[:, j:j + L], v("conv_w", 4 * c + j, 1), dst, ALU.mult, ALU.add))
                d.scalar_tensor_tensor(dst, src[:, 2:2 + L], v("conv_w", 4 * c + 2, 1), dst, ALU.mult,
                                       ALU.add).then_inc(conv_done, 1)

            def silu_of(c):
                d.wait_ge(conv_tanh, c + 1)
                at = slice(NMETA, L) if 4 <= c < 8 else slice(0, L)
                dst = BT[:, c, T0:T] if c < 4 else CT[:, c - 4, :] if c < 8 else xT[:, c - 8, T0:T]
                d.scalar_tensor_tensor(dst, convt[:, c % 2, at], 1.0, conv[:, c % 2, at], ALU.add,
                                       ALU.mult).then_inc(conv_fin, 1)

            d.wait_ge(consts_ready, 2)
            for c in range(4):
                if c + 2 >= NSPLIT:
                    lo_of(c + 2)
                conv_of(c)
                if c:
                    silu_of(c - 1)
            silu_of(3)
            lo_of(6)
            d.wait_ge(latent_trans, 1)
            for k in range(KKV):
                d.tensor_scalar(ckvT[:, k, :], bank[5 + k][:, 0:T], v("kv_norm", k, 1), None, ALU.mult)
            for k in range(KQ):
                last = d.tensor_scalar(qaT[:, k, :], bank[3 + k // 2][:, (k % 2) * SEQ:(k % 2 + 1) * SEQ],
                                       v("q_norm", k, 1), None, ALU.mult)
            last.then_inc(latentT_ready, 1)
            d.wait_ge(dt_ln, 1)
            link(d.scalar_tensor_tensor(dt[:, :], dtv[:, :], 0.0, dta[:, :], ALU.max, ALU.add))
            d.scalar_tensor_tensor(dA.rearrange("p (b h) -> p b h", b=NB), dt.rearrange("p (b h) -> p b h", b=NB), -1.0,
                                   negA[:, :].unsqueeze(1).to_broadcast([P, NB, HEADS_S]), ALU.mult,
                                   ALU.mult).then_inc(dA_ready, 1)
            for c in range(4, 8):
                if c == 4:
                    lo_of(7)
                conv_of(c)
                if c > 4:
                    silu_of(c - 1)
            silu_of(7)
            d.wait_ge(cum_done, 1)
            d.tensor_copy(AT[0:HEADS_S, :], bank[2][0:HEADS_S, 0:SEQ])
            d.tensor_copy(As[:, :], bank[3][:, 0:NB * HEADS_S]).then_inc(cum_read, 1)
            d.wait_ge(proj_read, U["q", 7] + 1)
            for b in range(2):
                qv = q_sb[:, b, :].rearrange("p (h r) -> p h r", h=MH)
                q1, q2 = qv[:, :, NOPE:NOPE + 16], qv[:, :, NOPE + 16:QH]
                cb = cosv[:, b + 1, :].unsqueeze(1).to_broadcast([P, MH, 16])
                sb_ = sinv[:, b + 1, :].unsqueeze(1).to_broadcast([P, MH, 16])
                o = 4 * b
                d.tensor_tensor(ropet[:, o], q1, cb, ALU.mult)
                d.tensor_tensor(ropet[:, o + 1], q2, sb_, ALU.mult)
                d.tensor_tensor(ropet[:, o + 2], q2, cb, ALU.mult)
                link(d.tensor_tensor(ropet[:, o + 3], q1, sb_, ALU.mult))
                d.tensor_tensor(q1, ropet[:, o], ropet[:, o + 1], ALU.subtract)
                last = d.tensor_tensor(q2, ropet[:, o + 2], ropet[:, o + 3], ALU.add)
            last.then_inc(q_roped, 1)
            d.wait_ge(AT_hi_ready, 1)
            d.tensor_tensor(AT_lo[:, :], AT[:, :], AT_hi[:, :], ALU.subtract).then_inc(AT_lo_ready, 1)

            def q_head(h):
                d.wait_ge(qk_done, h + 1)
                d.tensor_copy(qTh[0:QH, h % 2, :], bank[7][0:QH, 0:SEQ]).then_inc(qT_ready, 1)

            def max_head(h):
                d.wait_ge(scores_done, h + 1)
                if h >= 2:
                    d.wait_ge(pT_done, h - 1)
                d.tensor_tensor_reduce(out=probs[:, h % 2, 0, T0:2 * P], in0=bank[2][:, 0:L - P], in1=keymask[:, P:L],
                                       scale=1.0, scalar=NEG, op0=ALU.add, op1=ALU.max, accum_out=rmax[:, 0:1])
                link(d.tensor_tensor_reduce(out=probs[:, h % 2, 1, T0:T], in0=bank[2][:, L - P:2 * L - P], in1=keymask[:, :],
                                            scale=1.0, scalar=NEG, op0=ALU.add, op1=ALU.max, accum_out=rmax[:, 1:2]))
                d.tensor_scalar(nmax[:, h % 2, :], rmax[:, :], -1.0, None, ALU.mult).then_inc(scores_read, 1)

            def norm_head(h):
                d.wait_ge(exp_done, h + 1)
                link(d.reciprocal(rinv[:, :], rsum[:, h % 2, :]))
                d.tensor_scalar(probs[:, h % 2, 0, T0:2 * P], probs[:, h % 2, 0, T0:2 * P], rinv[:, 0:1], None, ALU.mult)
                d.tensor_scalar(probs[:, h % 2, 1, T0:T], probs[:, h % 2, 1, T0:T], rinv[:, 1:2], None,
                                ALU.mult).then_inc(probs_ready, 1)

            def attn_lo_of(i):
                d.wait_ge(attn_hi_ready, i + 1)
                d.tensor_tensor(attn_lo[:, i, :], bank[3][:, 0:SEQ], attn_hi[:, i, :], ALU.subtract).then_inc(pv_read, 1)

            lo_of(8)
            lo_of(9)
            q_head(0)
            max_head(0)
            d.wait_ge(zeros_ready, 2)
            for h in range(MH):
                if h + 1 < MH:
                    q_head(h + 1)
                norm_head(h)
                lo_of(8 + h + 2)
                if h and h % 2 == 0:
                    attn_lo_of(h // 2 - 1)
                if h + 1 < MH:
                    max_head(h + 1)
                conv_of(8 + h)
                if h:
                    silu_of(8 + h - 1)
                d.wait_ge(pT_done, h + 1)
                d.tensor_copy(pT[:, 512:640], bank[5][:, 0:P]).then_inc(pTb_ready, 1)
            attn_lo_of(KD - 1)
            silu_of(8 + MH - 1)
            for g in range(GROUPS):
                d.wait_ge(cb_done, g + 1)
                ba, bb = bank[4 + 2 * (g % 2)], bank[5 + 2 * (g % 2)]
                d.tensor_copy(CBm[:, g, 0:SEQ], ba[:, 0:SEQ])
                d.tensor_tensor(CBm[:, g, SEQ:2 * SEQ], ba[:, SEQ:2 * SEQ], tri[:, :], ALU.mult)
                d.tensor_tensor(CBm[:, g, 2 * SEQ:2 * SEQ + P], bb[:, 0:P], tri[:, 0:P], ALU.mult).then_inc(cb_read, 1)

            def diff_of(c):
                d.wait_ge(acum_done, c + 1)
                if c >= 2:
                    d.wait_ge(ssdy_done, c - 1)
                for b, (lo, at) in enumerate(DECAY_AT):
                    col = b * HEADS_S + 2 * c
                    last = d.tensor_scalar(decay[:, c % 2, 0, at:at + SEQ - lo], bank[2][:, lo:SEQ], As[:, col:col + 1],
                                           0.0, ALU.subtract, ALU.min)
                last.then_inc(diff_ready, 1)

            def xdt_of(c):
                d.wait_ge(xtr_done, c + 1)
                d.tensor_tensor(xdt[:, c % 2, :, :].rearrange("p b (j t) -> p b j t", j=2),
                                bank[6][:, 0:T].rearrange("p (b j t) -> p b j t", b=NB, j=2),
                                dt.rearrange("p (b h) -> p b h", b=NB)[:, :, 2 * c:2 * c + 2].unsqueeze(3)
                                .to_broadcast([P, NB, 2, VH]), ALU.mult).then_inc(xdt_ready, 1)

            def sc_of(c):
                d.wait_ge(decay_exp, c + 1)
                d.tensor_tensor(decay[:, c % 2, :, :], decay[:, c % 2, :, :],
                                CBm[:, c // CHUNKS_PER_GROUP, :].unsqueeze(1).to_broadcast([P, 2, 640]),
                                ALU.mult).then_inc(sc_ready, 1)

            def var_group(g):
                d.wait_ge(gsum_done, CHUNKS_PER_GROUP * (g + 1))
                d.tensor_scalar(var_g[:, g * SEQ:(g + 1) * SEQ], bank[7][:, 0:SEQ], 1.0 / 512, EPS, ALU.mult,
                                ALU.add).then_inc(gsum_read, 1)

            diff_of(0)
            xdt_of(0)
            sc_of(0)
            for c in range(NX):
                if c + 1 < NX:
                    diff_of(c + 1)
                    xdt_of(c + 1)
                lo_of(PZ + c + 2)
                if c + 1 < NX:
                    sc_of(c + 1)
                d.wait_ge(ssdy_done, c + 1)
                if c:
                    d.wait_ge(y2_ready, c)
                d.scalar_tensor_tensor(yv, xT[:, c, P:T], v("d_skip", c, 1), bank[3 + 2 * (c % 2)][:, 0:SEQ], ALU.mult,
                                       ALU.add).then_inc(ssdy_read, 1)
                d.wait_ge(ssdy_read, c + 1)
                d.wait_ge(zw_ready, c + 1)
                d.tensor_tensor(y2T[:, c, :], yv, zw, ALU.mult).then_inc(y2_ready, 1)
                if c and c % CHUNKS_PER_GROUP == 0:
                    var_group(c // CHUNKS_PER_GROUP - 1)
            def merge_attention(m):
                if m == 0:
                    d.wait_ge(proj_read, len(UNITS))
                d.wait_ge(out_done, m + 1)
                d.scalar_tensor_tensor(mT[:, m, :], gt[:, KD + m, :], 1.0, bank[2 + m % 2][:, 0:SEQ], ALU.add,
                                       ALU.mult).then_inc(merged, 1)

            for u in range(PSO - PG):
                lo_of(PG + u + 2)
                if u == 2:
                    var_group(GROUPS - 1)
                g, stage = norm_stage(u)
                chunks = [] if g is None else range(CHUNKS_PER_GROUP * g, CHUNKS_PER_GROUP * (g + 1))
                if stage is not None:
                    val, rs, tmp = (t[:, g * SEQ:(g + 1) * SEQ] for t in (var_g, rstd_g, tmp_g))
                if stage == 0:
                    d.wait_ge(gsum_read, g + 1)
                    rsqrt_guess(rs, val)
                    newton(rs, val, tmp)
                elif stage == 1:
                    newton(rs, val, tmp)
                    newton(rs, val, tmp)
                elif stage == 2:
                    for c in chunks:
                        d.scalar_tensor_tensor(y2T[:, c, :], y2T[:, c, :], v("ssd_norm", c, 1), rs, ALU.mult,
                                               ALU.mult).then_inc(yn_ready, 1)
                if u >= 16:
                    merge_attention(u - 16)
            for m in range(KD):
                for p in (PSO + 2 * m + 2, PSO + 2 * m + 3):
                    if p < len(PIECES):
                        lo_of(p)
                d.wait_ge(out_done, KD + m + 1)
                link(d.scalar_tensor_tensor(mtmp[:, m % 2, :], gt[:, m, :], 1.0, bank[2 + m % 2][:, 0:SEQ], ALU.add, ALU.mult))
                d.tensor_tensor(mT[:, m, :], mT[:, m, :], mtmp[:, m % 2, :], ALU.add).then_inc(merged, 1)
            d.wait_ge(xres_in, 32)
            d.wait_ge(rows_in, 16)

            def residual_half(b, n):
                d.wait_ge(wout_done, 2 * b + n + 1)
                half = slice(n * 512, (n + 1) * 512)
                d.scalar_tensor_tensor(h1[:, b, half], bank[4 + 2 * n + b][:, :], 0.5, xres[:, b, half], ALU.mult,
                                       ALU.add).then_inc(h1_ready, 1)
                d.wait_ge(h1_ready, 2 * b + n + 1)
                d.tensor_tensor(xn[:, b, half], h1[:, b, half], nf[:, half], ALU.mult).then_inc(xn_ready, 1)

            def rstd_block(b):
                d.wait_ge(h1_squared, 2 * (b + 1))
                link(d.tensor_tensor(ssh[:, b:b + 1], ssh4[:, b, 0:1], ssh4[:, b, 1:2], ALU.add))
                rstd(rsh[:, b:b + 1], ssh[:, b:b + 1], D, EPS)
                d.tensor_copy(rsn[:, b:b + 1], rsh[:, b:b + 1]).then_inc(rsn_ready, 1)

            def top4(b):
                d.wait_ge(logits_done, b + 1)
                link(d.scalar_tensor_tensor(lg[:, b, :], bank[4 + b][:, 0:E], rsh[:, b:b + 1], v("b_router"), ALU.mult, ALU.add))
                link(d.max(mx8[:, b, :], lg[:, b, :]))
                link(d.max_index(idx[:, 8 * b:8 * b + 8], mx8[:, b, :], lg[:, b, :]))
                d.tensor_scalar(nm4[:, b:b + 1], mx8[:, b, 0:1], -1.0, None, ALU.mult).then_inc(top_ready, 1)
                link(d.tensor_copy(idxf[:, b, :], idx[:, 8 * b:8 * b + 8]))
                link(d.tensor_tensor(chosen[:, b, :, :], iota_e[:, :].unsqueeze(1).to_broadcast([P, TOPK, E]),
                                     idxf[:, b, 0:TOPK].unsqueeze(2).to_broadcast([P, TOPK, E]), ALU.is_equal))
                d.tensor_reduce(mask[:, b, :], chosen[:, b, :, :].rearrange("p j e -> p e j"), AX.X, ALU.add).then_inc(mask_ready, 1)

            def weights(b):
                d.wait_ge(top_exp, b + 1)
                link(d.reciprocal(r4[:, b:b + 1], s4[:, b:b + 1]))
                link(d.tensor_scalar(e4[:, b, :], e4[:, b, :], r4[:, b:b + 1], None, ALU.mult))
                link(d.tensor_tensor(chosen[:, b, :, :], chosen[:, b, :, :],
                                     e4[:, b, :].unsqueeze(2).to_broadcast([P, TOPK, E]), ALU.mult))
                link(d.tensor_reduce(PW[:, 2 + b, 0:E], chosen[:, b, :, :].rearrange("p j e -> p e j"), AX.X, ALU.add))

            residual_half(0, 0)
            residual_half(0, 1)
            rstd_block(0)
            residual_half(1, 0)
            d.wait_ge(moe_zero, 3)
            top4(0)
            residual_half(1, 1)
            rstd_block(1)
            weights(0)
            top4(1)
            weights(1)
            d.tensor_copy(wpad[:, :, 0:E], PW[:, 2:4, 0:E]).then_inc(route_ready, 1)
            d.wait_ge(pos_done, 1)
            ps = bank[6][:, 0:2 * E].rearrange("p (b e) -> p b e", b=2)
            link(d.tensor_tensor(PW[:, 0:2, 0:E], ps, mask[:, :, :], ALU.mult))
            link(d.tensor_scalar(PW[:, 0:2, 0:E], PW[:, 0:2, 0:E], -1.0, None, ALU.add))

            def count():
                d.wait_ge(pos_done, 2)
                link(d.tensor_reduce(cmax[:, :], bank[4][:, 0:E], AX.X, ALU.max))
                d.tensor_copy(cmax_i[:, :], cmax[:, :]).then_inc(count_ready, 1)

            PER_EXPERT = 2
            PER_ROUND = 1 + E * PER_EXPERT + 1

            def expert_round(r, first):
                def link_at(n):
                    def link(ins):
                        nonlocal n
                        n = n + 1
                        ins.then_inc(moe_step, 1)
                        d.wait_ge(moe_step, n)
                    return link

                def pick(e, link, gathers):
                    link(d.tensor_copy(pw[:, :], PW[:, :, bass.ds(e, 1)].rearrange("p i o -> p (i o)")))
                    if gathers is not None:
                        d.wait_ge(gather_done, gathers)
                    d.tensor_scalar(hot[:, 0, :], iota_slot[:, :], pw[:, 0:1], None, ALU.is_equal)
                    d.tensor_scalar(hot[:, 1, :], iota_slot[:, :], pw[:, 1:2], None, ALU.is_equal).then_inc(hot_ready, 1)

                pick(0, link_at(r * PER_ROUND), None if first else r * (E + 1))
                d.tensor_copy(bsel[:, :], ident[:, 0:1].to_broadcast([P, SLOTS])).then_inc(bsel_ready, 1)
                if first:
                    count()
                with d.Fori(0, E) as e:
                    t = r * E + e
                    link = link_at(r * PER_ROUND + 1 + e * PER_EXPERT)
                    for b in range(2):
                        last = d.tensor_scalar(hotw[:, b, :, :], iota_slot[:, :].unsqueeze(1).to_broadcast([P, 2, SLOTS]),
                                               pw[:, b:b + 1], pw[:, 2 + b:3 + b], ALU.is_equal, ALU.mult)
                    last.then_inc(hotw_ready, 1)
                    d.wait_ge(hotw_ready, t + 1)
                    pick(e + 1, link, r * (E + 1) + e + 1)
                    d.wait_ge(up_done, t + 1)
                    for i in range(2):
                        hv = bank[4 + i][:, :].rearrange("p (f o) -> p f o", o=2)
                        last = d.tensor_scalar(glu[:, i * 256:(i + 1) * 256], hv[:, :, 0], LIMIT, None, ALU.min)
                    last.then_inc(glu_ready, 1)
                    for i in range(2):
                        hv = bank[4 + i][:, :].rearrange("p (f o) -> p f o", o=2)
                        last = d.tensor_scalar(lin[:, i * 256:(i + 1) * 256], hv[:, :, 1], LIMIT, -LIMIT, ALU.min, ALU.max)
                    last.then_inc(up_read, 1)
                    d.tensor_copy(bsel[:, :], ident[:, bass.ds(e + 1, 1)].to_broadcast([P, SLOTS])).then_inc(bsel_ready, 1)
                    d.wait_ge(up_read, t + 1)
                    link(d.scalar_tensor_tensor(lin[:, :], lin[:, :], 1.0, glu[:, :], ALU.add, ALU.mult))
                    d.wait_ge(sig_ready, t + 1)
                    d.scalar_tensor_tensor(act[:, :], sig[:, :], 1.0, lin[:, :], ALU.add, ALU.mult).then_inc(act_ready, 1)
                    d.wait_ge(scat_trans, t + 1)
                    d.tensor_copy(scat[0:SLOTS, 0, :], bank[5][0:SLOTS, 0:SEQ])
                    d.tensor_copy(scat[SLOTS:P, 1, :], bank[5][SLOTS:P, 0:SEQ]).then_inc(scat_ready, 1)

            expert_round(0, True)
            cm = d.value_load(cmax_i[0:1, 0:1], min_val=0, max_val=SEQ)
            with d.If(cm > SLOTS):
                with d.Fori(1, SEQ // SLOTS) as r:
                    d.tensor_scalar(PW[:, 0:2, 0:E], PW[:, 0:2, 0:E], -float(SLOTS), None, ALU.add).then_inc(moe_step, 1)
                    d.wait_ge(moe_step, r * PER_ROUND)
                    expert_round(r, False)
            for b in range(2):
                d.wait_ge(scattered, b + 1)
                for n in range(2):
                    last = d.tensor_tensor(h1[:, b, n * 512:(n + 1) * 512], bank[2 * b + n][:, :],
                                           h1[:, b, n * 512:(n + 1) * 512], ALU.add)
                last.then_inc(h2_ready, 1)
            for b in range(2):
                d.wait_ge(h2_squared, b + 1)
                rstd(rsh[:, b:b + 1], ssh[:, b:b + 1], D, EPS)
                d.scalar_tensor_tensor(fin[:, b, :], h1[:, b, :], rsh[:, b:b + 1], nfin, ALU.mult, ALU.mult).then_inc(y_ready, 1)

        @block.tensor
        def _(pe):
            def mm(o, lhsT, rhs, start=True, stop=True):
                return pe.matmul(o, lhsT, rhs, start=start, stop=stop)

            def take(name):
                pe.wait_ge(*arrived(name))
                return slab(name)

            def split_mm(o, p, hi, lo, start, stop):
                pe.wait_ge(lo_ready, p + 1)
                ws = split[p % NSPLIT]
                for k in range(KD):
                    mm(o, ws[:, 0, k, :], hi(k), start and k == 0, False)
                    mm(o, ws[:, 0, k, :], lo(k), False, False)
                    last = mm(o, ws[:, 1, k, :], hi(k), False, stop and k == KD - 1)
                return last

            def unit(kind, i):
                u = U[kind, i]
                if u >= 2:
                    pe.wait_ge(proj_read, u - 1)
                return bank[u % 2]

            pe.wait_ge(consts_ready, 1)
            for i in range(6):
                b, k0 = ORDER[i // 2], 4 * (i % 2)
                pe.wait_ge(hn_ready, i // 2 + 1)
                for k in range(4):
                    last = pe.transpose(bank[i][:, k * P:(k + 1) * P], xtok[:, b, (k0 + k) * P:(k0 + k + 1) * P], ident[:, :])
                last.then_inc(hn_trans, 1)
            wsl = take("dkv").rearrange("p (k n) -> p k n", k=KD)
            for i, b in enumerate(ORDER):
                pe.wait_ge(hnT_ready, 6 if i else 2)
                ps = bank[i % 2]
                if i >= 2:
                    ps = unit("dkv", b)
                for k in range(KD):
                    last = mm(ps[:, 0:DKV], hnT[:, k, b * P:(b + 1) * P], wsl[:, k, :], k == 0, k == KD - 1)
                last.then_inc(proj_done, 1)
            wsl = take("qa").rearrange("p (k n) -> p k n", k=KD)
            for b in (1, 2):
                ps = unit("qa", b)
                for k in range(KD):
                    last = mm(ps[:, 0:QL], hnT[:, k, b * P:(b + 1) * P], wsl[:, k, :], k == 0, k == KD - 1)
                last.then_inc(proj_done, 1)

            def feature_unit(kind, i, p, t0):
                ps = unit(kind, i)
                split_mm(ps[:, 0:T - t0], p, lambda k: hn_hi[:, k, t0:T], lambda k: hn_lo[:, k, t0:T], True,
                         True).then_inc(proj_done, 1)

            pe.wait_ge(hn_lo_ready, 6)
            for c in range(5):
                feature_unit("cv", c, c, T0)
            pe.wait_ge(latent_ready, 1)
            for b in range(NB):
                for k in range(KKV):
                    pe.transpose(bank[5 + k][:, b * P:(b + 1) * P], ckk[:, b, k * P:(k + 1) * P], ident[:, :])
                pe.transpose(bank[7][0:QH, b * P:(b + 1) * P], ckk[:, b, KVL:KVL + QH], ident[:, :])
            for b in range(2):
                for k in range(KQ):
                    last = pe.transpose(bank[3 + k // 2][:, (k % 2) * SEQ + b * P:(k % 2) * SEQ + (b + 1) * P],
                                        qa[:, b, k * P:(k + 1) * P], ident[:, :])
            last.then_inc(latent_trans, 1)
            for c in range(5, 8):
                feature_unit("cv", c, c, T0)
            pe.wait_ge(latentT_ready, 1)
            pe.wait_ge(dA_ready, 1)
            pe.wait_ge(consts_ready, 2)
            dAb = [dA[:, b * HEADS_S:(b + 1) * HEADS_S] for b in range(NB)]
            mm(bank[2][0:HEADS_S, 0:SEQ], dAb[0], metarows[:, :], True, False)
            mm(bank[2][0:HEADS_S, P:SEQ], dAb[2], tri[:, 0:P], False, False)
            mm(bank[2][0:HEADS_S, 0:SEQ], dAb[1], tri[:, :], False, True)
            for b, mats in enumerate([[trimeta], [metarows, tri], [metarows, ones, tri]]):
                for i, m in enumerate(mats):
                    last = mm(bank[3][:, b * HEADS_S:(b + 1) * HEADS_S], m[:, 0:P], dAb[i], i == 0, i == len(mats) - 1)
            last.then_inc(cum_done, 1)
            for half in range(2):
                wsl = take(f"uq{half}").rearrange("p (k n) -> p k n", k=KQ)
                for i in range(4 * half, 4 * half + 4):
                    b, part = i % 2, (i // 2) % 2
                    ps = unit("q", i)
                    for k in range(KQ):
                        last = mm(ps[:, 0:QL], qaT[:, k, b * P:(b + 1) * P], wsl[:, k, part * QL:(part + 1) * QL],
                                  k == 0, k == KQ - 1)
                    last.then_inc(proj_done, 1)
            ukv = take("ukv").rearrange("p (k n) -> p k n", k=KKV)
            for i in range(6):
                b, n = i // 2, i % 2
                ps = unit("v", i)
                for k in range(KKV):
                    last = mm(ps[:, :], ckvT[:, k, b * P:(b + 1) * P], ukv[:, k, 1024 + n * 512:1024 + (n + 1) * 512],
                              k == 0, k == KKV - 1)
                last.then_inc(proj_done, 1)

            def qk_head(h):
                if h >= 1:
                    pe.wait_ge(kT_ready, h)
                    pe.wait_ge(qT_ready, h)
                for k in range(KKV):
                    mm(bank[6][0:NOPE, 0:L], ukv[:, k, h * NOPE:(h + 1) * NOPE], ckvT[:, k, T0:T], k == 0, k == KKV - 1)
                for b in range(2):
                    last = pe.transpose(bank[7][0:QH, b * P:(b + 1) * P], q_sb[:, b, h * QH:(h + 1) * QH], ident[:, :])
                last.then_inc(qk_done, 1)

            def scores_head(h):
                pe.wait_ge(kT_ready, h + 1)
                pe.wait_ge(qT_ready, h + 1)
                if h >= 1:
                    pe.wait_ge(scores_read, h)
                mm(bank[2][:, 0:L - P], qTh[0:QH, h % 2, 0:P], kTh[0:QH, h % 2, 0:L - P])
                mm(bank[2][:, L - P:2 * L - P], qTh[0:QH, h % 2, P:SEQ], kTh[0:QH, h % 2, :]).then_inc(scores_done, 1)

            def probs_trans(h):
                pe.wait_ge(probs_ready, h + 1)
                if h:
                    pe.wait_ge(pTa_ready, h)
                    pe.wait_ge(pTb_ready, h)
                for b in range(2):
                    for qb in range(2):
                        pe.transpose(bank[4][:, b * SEQ + qb * P:b * SEQ + (qb + 1) * P],
                                     probs[:, h % 2, qb, b * P:(b + 1) * P], ident[:, :])
                pe.transpose(bank[5][:, 0:P], probs[:, h % 2, 1, 2 * P:T], ident[:, :]).then_inc(pT_done, 1)

            def pv_head(h):
                pe.wait_ge(pTa_ready, h + 1)
                pe.wait_ge(pTb_ready, h + 1)
                if h >= 2 and h % 2 == 0:
                    pe.wait_ge(pv_read, h // 2)
                o = bank[3][(h % 2) * VH:(h % 2 + 1) * VH, 0:SEQ]
                vh = [V[:, b, h * VH:(h + 1) * VH] for b in range(NB)]
                mm(o, vh[0], pT[:, 0:SEQ], True, False)
                mm(o[:, P:SEQ], vh[2], pT[:, 2 * SEQ:2 * SEQ + P], False, False)
                mm(o, vh[1], pT[:, SEQ:2 * SEQ], False, True).then_inc(pv_done, 1)

            pe.wait_ge(kpeT_ready, 2)
            pe.wait_ge(q_roped, 1)
            qk_head(0)
            pe.wait_ge(cum_read, 1)
            scores_head(0)
            for h in range(MH):
                if h + 1 < MH:
                    qk_head(h + 1)
                feature_unit("cv", 8 + h, 8 + h, T0)
                if h:
                    pv_head(h - 1)
                if h + 1 < MH:
                    scores_head(h + 1)
                probs_trans(h)
            feature_unit("z", 0, PZ, P)
            pv_head(MH - 1)

            pe.wait_ge(pv_read, KD)
            for g in range(GROUPS):
                if g >= 2:
                    pe.wait_ge(cb_read, g - 1)
                ba, bb = bank[4 + 2 * (g % 2)], bank[5 + 2 * (g % 2)]
                mm(ba[:, 0:SEQ], BT[:, g, 0:P], CT[:, g, :])
                mm(ba[:, SEQ:2 * SEQ], BT[:, g, P:2 * P], CT[:, g, :])
                mm(bb[:, 0:P], BT[:, g, 2 * P:T], CT[:, g, P:SEQ]).then_inc(cb_done, 1)

            def acum_of(c):
                if c:
                    pe.wait_ge(diff_ready, c)
                    pe.wait_ge(diff2_ready, c)
                for j in range(2):
                    row = head_row[:, 2 * c + j:2 * c + j + 1].to_broadcast([P, P])
                    mm(bank[2 + 2 * j][:, 0:SEQ], row, AT_hi[:, :], True, False)
                    last = mm(bank[2 + 2 * j][:, 0:SEQ], row, AT_lo[:, :], False, True)
                last.then_inc(acum_done, 1)

            def xtr_of(c):
                if c:
                    pe.wait_ge(xdt_ready, c)
                for b in range(NB):
                    last = pe.transpose(bank[6][:, b * P:(b + 1) * P], xT[:, c, b * P:(b + 1) * P], ident[:, :])
                last.then_inc(xtr_done, 1)

            def gsum_of(c):
                pe.wait_ge(ysq_ready, c + 1)
                if c and c % CHUNKS_PER_GROUP == 0:
                    pe.wait_ge(gsum_read, c // CHUNKS_PER_GROUP)
                mm(bank[7][:, 0:SEQ], ones[:, :], ysq[:, c % 2, :], c % CHUNKS_PER_GROUP == 0,
                   c % CHUNKS_PER_GROUP == CHUNKS_PER_GROUP - 1).then_inc(gsum_done, 1)

            pe.wait_ge(AT_lo_ready, 1)
            pe.wait_ge(cb_read, GROUPS - 1)
            acum_of(0)
            pe.wait_ge(cb_read, GROUPS)
            pe.wait_ge(conv_fin, 24)
            xtr_of(0)
            for c in range(NX):
                if c + 1 < NX:
                    acum_of(c + 1)
                    xtr_of(c + 1)
                if c + 1 < NX:
                    feature_unit("z", c + 1, PZ + c + 1, P)
                else:
                    feature_unit("g", 0, PG, P)
                pe.wait_ge(sc_ready, c + 1)
                if c >= 2:
                    pe.wait_ge(ssdy_read, c - 1)
                for b, at, lo in ((0, 0, 0), (2, 2 * SEQ, P), (1, SEQ, 0)):
                    for j in range(2):
                        last = mm(bank[3 + 2 * (c % 2)][j * VH:(j + 1) * VH, lo:SEQ], xdt[:, c % 2, b, j * VH:(j + 1) * VH],
                                  decay[:, c % 2, j, at:at + SEQ - lo], b == 0, b == 1)
                last.then_inc(ssdy_done, 1)
                if c:
                    gsum_of(c - 1)
            for c in range(1, 16):
                if c == 2:
                    gsum_of(NX - 1)
                feature_unit("g", c, PG + c, P)
            pe.wait_ge(ssdy_read, NX)
            for m in range(KD):
                if m >= 2:
                    pe.wait_ge(merged, m - 1)
                split_mm(bank[2 + m % 2][:, 0:SEQ], PWO + m, lambda k: attn_hi[:, k, :], lambda k: attn_lo[:, k, :], True,
                         True).then_inc(out_done, 1)
            pe.wait_ge(y2_lo_ready, KD)
            for m in range(KD):
                pe.wait_ge(merged, KD + m - 1)
                o = bank[2 + m % 2][:, 0:SEQ]
                split_mm(o, PSO + 2 * m, lambda k: y2_hi[k], lambda k: y2_lo[:, k, :], True, False).then_inc(so_half, 1)
                if m == 0:
                    pe.wait_ge(y2_lo_ready, NX)
                split_mm(o, PSO + 2 * m + 1, lambda k: y2_hi[KD + k], lambda k: y2_lo[:, KD + k, :], False,
                         True).then_inc(out_done, 1)
            pe.wait_ge(gsum_read, GROUPS)
            wout = [take(f"wout{n}").rearrange("p (k n) -> p k n", k=KD) for n in range(2)]

            def wout_unit(b, n, ks):
                for k in ks:
                    if (b, n) == (0, 0) and k >= KD - 2:
                        pe.wait_ge(merged, KD + k + 1)
                    elif (b, n, k) == (0, 0, 0):
                        pe.wait_ge(merged, 2 * KD - 2)
                    last = mm(bank[4 + 2 * n + b][:, :], mT[:, k, b * P:(b + 1) * P], wout[n][:, k, :], k == 0, k == KD - 1)
                return last

            def xn_transposes(b, n):
                pe.wait_ge(xn_ready, 2 * b + n + 1)
                for k in range(4):
                    last = pe.transpose(bank[2 * b + n][:, k * P:(k + 1) * P],
                                        xn[:, b, (4 * n + k) * P:(4 * n + k + 1) * P], ident[:, :])
                last.then_inc(xn_trans, 1)

            def logits(b):
                pe.wait_ge(h1_ready, 2 * b + 1)
                pe.wait_ge(xnT_ready, 2 * (b + 1))
                for k in range(KD):
                    last = mm(bank[4 + b][:, 0:E], xnT[:, b, k, :], v("w_router", k * E, E), k == 0, k == KD - 1)
                last.then_inc(logits_done, 1)

            wout_unit(0, 0, range(KD)).then_inc(wout_done, 1)
            wout_unit(0, 1, range(KD)).then_inc(wout_done, 1)
            xn_transposes(0, 0)
            wout_unit(1, 0, range(KD)).then_inc(wout_done, 1)
            xn_transposes(0, 1)
            wout_unit(1, 1, range(0, 3))
            logits(0)
            wout_unit(1, 1, range(3, KD)).then_inc(wout_done, 1)
            xn_transposes(1, 0)
            xn_transposes(1, 1)
            logits(1)
            pe.wait_ge(mask_ready, 1)
            mm(bank[6][:, 0:E], tri[:, 0:P], mask[:, 0, :])
            mm(bank[6][:, E:2 * E], ones[:, :], mask[:, 0, :], True, False)
            mm(bank[4][:, 0:E], ones[:, :], mask[:, 0, :], True, False)
            pe.wait_ge(mask_ready, 2)
            mm(bank[6][:, E:2 * E], tri[:, 0:P], mask[:, 1, :], False, True).then_inc(pos_done, 1)
            mm(bank[4][:, 0:E], ones[:, :], mask[:, 1, :], False, True).then_inc(pos_done, 1)
            pe.wait_ge(route_ready, 1)
            for b in range(2):
                last = pe.transpose(bank[5][:, b * P:(b + 1) * P], wpad[:, b, :], ident[:, :])
            last.then_inc(w_trans, 1)
            def gather(n):
                pe.wait_ge(hot_ready, n)
                for b in range(2):
                    for j in range(2):
                        last = mm(bank[7][j * SLOTS:(j + 1) * SLOTS, :], hot[:, b, :], xn[:, b, j * 512:(j + 1) * 512], b == 0, b == 1)
                last.then_inc(gather_done, 1)

            def gather_trans(n):
                pe.wait_ge(xg_ready, n)
                for j in range(4):
                    last = pe.transpose(bank[7][:, j * P:(j + 1) * P], xg[:, j * P:(j + 1) * P], ident[:, :])
                last.then_inc(xg_trans, 1)

            FIRST = 0
            pe.wait_ge(xn_scaled, 2)
            gather(1)
            pe.wait_ge(wT_ready, 1)
            pe.wait_ge(bias_in, 32)
            for b in range(2):
                for n in range(2):
                    mm(bank[2 * b + n][:, :], wTs[:, b * P:(b + 1) * P], b2all[:, n * 512:(n + 1) * 512], True, False)

            def scatter(stop):
                for b in range(2):
                    for n in range(2):
                        last = mm(bank[2 * b + n][:, :], scat[:, n, b * P:(b + 1) * P], ob[:, :], False, stop)
                    if stop:
                        last.then_inc(scattered, 1)

            def expert(e, r, pair, odd):
                t, g = r * E + e, r * (E + 1) + e + 1
                pe.wait_ge(xgT_ready, g)
                pe.wait_ge(bsel_ready, g)
                pe.wait_ge(actT_ready, t + 1)
                pe.wait_ge(scat_ready, t + 1)
                for i in range(2):
                    for j in range(2):
                        mm(bank[4 + i][j * SLOTS:(j + 1) * SLOTS, :], bsel[:, :],
                           b1all[:, j * 1024 + i * 512:j * 1024 + (i + 1) * 512], True, False)
                for k in range(KD):
                    if k >= len(w1_odd):
                        weights = w1_sb[k]
                        pe.wait_ge(w1_in[k], 16 * (t + 1))
                    elif odd:
                        weights = w1_odd[k]
                        pe.wait_ge(w1_odd_in[k], 16 * (pair + 1))
                    else:
                        weights = w1_sb[k]
                        pe.wait_ge(w1_in[k], 16 * (pair + 1))
                    for i in range(2):
                        for j in range(2):
                            last = mm(bank[4 + i][j * SLOTS:(j + 1) * SLOTS, :],
                                      xgT[:, k % 4, (k // 4) * SLOTS:(k // 4 + 1) * SLOTS],
                                      weights[:, j * 1024 + i * 512:j * 1024 + (i + 1) * 512], False, k == KD - 1)
                    if k < KD - 1:
                        last.then_inc(chunk_used, 1)
                last.then_inc(up_done, 1)
                gather(g + 1)
                pe.wait_ge(ob_ready, t + 1)
                scatter(False)
                gather_trans(g + 1)
                pe.wait_ge(hotw_ready, t + 1)
                pe.wait_ge(up_read, t + 1)
                for b in range(2):
                    last = pe.transpose(bank[5][:, b * P:(b + 1) * P], hotw[:, b, :, :].rearrange("p i s -> p (i s)"), ident[:, :])
                last.then_inc(scat_trans, 1)
                pe.wait_ge(act_ready, t + 1)
                for j in range(4):
                    last = pe.transpose(bank[4][:, j * P:(j + 1) * P], act[:, j * P:(j + 1) * P], ident[:, :])
                last.then_inc(act_trans, 1)
                pe.wait_ge(actT_ready, t + 2)
                for k in range(KD):
                    if k % 2 == 0:
                        pe.wait_ge(w2_in[k // 2], 16 * (t + 1))
                    for j in range(2):
                        last = mm(bank[6][j * SLOTS:(j + 1) * SLOTS, :], actT[:, k % 4, (k // 4) * SLOTS:(k // 4 + 1) * SLOTS],
                                  w2_sb[k // 2][:, k % 2, j * 512:(j + 1) * 512], k == 0, k == KD - 1)
                    if k % 2 and k < KD - 1:
                        last.then_inc(chunk_used, 1)
                last.then_inc(down_done, 1)

            def expert_round(r):
                if r is FIRST:
                    pe.wait_ge(count_ready, 1)
                else:
                    gather(r * (E + 1) + 1)
                gather_trans(r * (E + 1) + 1)
                with pe.Fori(0, E // 2) as i:
                    for odd in (0, 1):
                        expert(2 * i + odd, r, r * (E // 2) + i, odd)

            expert_round(FIRST)
            pe.wait_ge(count_ready, 1)
            cm = pe.value_load(cmax_i[0:1, 0:1], min_val=0, max_val=SEQ)
            with pe.If(cm > SLOTS):
                with pe.Fori(1, SEQ // SLOTS) as r:
                    expert_round(r)
                pe.wait_ge(ob_ready, E * (SEQ // SLOTS) + 1)
                pe.wait_ge(scat_ready, E * (SEQ // SLOTS) + 1)
            pe.wait_ge(ob_ready, E + 1)
            pe.wait_ge(scat_ready, E + 1)
            scatter(True)


def pack_slabs(inp):
    import numpy as np
    w_in, w_ukv = inp["w_in"][0], inp["w_ukv"][0].reshape(KVL, MH, NOPE + VH)

    def rows(a):
        return a.reshape(-1, P, a.shape[1]).transpose(1, 0, 2).reshape(P, -1)

    parts = {"dkv": np.concatenate([w_in[:, DT0:DT0 + HEADS_S], w_in[:, KV0:KV0 + KVL + ROPE]], axis=1),
             "qa": w_in[:, QA0:QA0 + QL], "B": w_in[:, B0:B0 + 512], "C": w_in[:, C0:C0 + 512],
             "ukv": np.concatenate([w_ukv[:, :, :NOPE].reshape(KVL, -1), w_ukv[:, :, NOPE:].reshape(KVL, -1)], axis=1)}
    for i in range(2):
        parts[f"uq{i}"] = inp["w_uq"][0][:, 768 * i:768 * (i + 1)]
        parts[f"wo{i}"] = inp["w_o"][0][:, 512 * i:512 * (i + 1)]
        parts[f"wout{i}"] = inp["w_out"][0][:, 512 * i:512 * (i + 1)]
    for i in range(4):
        parts[f"xs{i}"] = w_in[:, XS0 + 512 * i:XS0 + 512 * (i + 1)]
        parts[f"z{i}"] = w_in[:, Z0 + 512 * i:Z0 + 512 * (i + 1)]
        parts[f"g{i}"] = w_in[:, G0 + 512 * i:G0 + 512 * (i + 1)]
        parts[f"so{i}"] = inp["w_ssd_out"][0][:, 256 * i:256 * (i + 1)]
    return np.concatenate([rows(parts[name]) for name, _ in SLABS], axis=1)


def pack_vectors(inp):
    import numpy as np

    def cols(a):
        return a.reshape(-1, P).T

    pos = np.arange(L, dtype=np.float32)
    inv = np.float32(10000.0) ** (-np.arange(0, ROPE, 2, dtype=np.float32) / np.float32(ROPE))
    ang = np.concatenate([np.zeros((T0, 16), np.float32), pos[:, None] * inv[None, :]])
    blocks = {
        "norm_mix": cols(inp["norm_mix"][0]),
        "conv_w": np.roll(inp["conv_w"][0].reshape(4, 24, P), 8, axis=1).transpose(2, 1, 0).reshape(P, -1),
        "conv_b": np.roll(cols(inp["conv_b"][0]), 8, axis=1), "ssd_norm": cols(inp["ssd_norm"][0]),
        "d_skip": cols(np.repeat(inp["d_skip"][0], 64)), "q_norm": cols(inp["q_norm"][0]),
        "kv_norm": cols(inp["kv_norm"][0]),
        "cos": np.cos(ang).reshape(NB, P, 16).transpose(1, 0, 2).reshape(P, -1),
        "sin": np.sin(ang).reshape(NB, P, 16).transpose(1, 0, 2).reshape(P, -1),
        "w_router": inp["w_router"][0].reshape(KD, P, E).transpose(1, 0, 2).reshape(P, -1),
    }
    for name in ("dt_bias", "a_log", "b_router"):
        blocks[name] = np.broadcast_to(inp[name][0][None, :], (P, E))
    return np.concatenate([blocks[name] for name in VEC], axis=1).astype(np.float32)


def kernel(**inputs):
    import numpy as np
    import concourse.bacc as bacc
    from concourse.bass_utils import run_bass_kernel_spmd

    inp = {k: np.asarray(a) for k, a in inputs.items()}
    arrays = {
        "x": inp["x"][0], "meta": inp["meta_tokens"], "slabs": pack_slabs(inp), "vecs": pack_vectors(inp),
        "rows": np.broadcast_to(np.concatenate([inp["norm_ffn"][0], inp["norm_final"]])[None, :], (P, 2 * D)),
        "w1": inp["w_mlp1"].reshape(E * D, 2 * DE), "b1": inp["b_mlp1"][0],
        "w2": inp["w_mlp2"].reshape(E * DE, D), "b2": inp["b_mlp2"][0],
    }
    arrays = {f"{k}_dram": np.ascontiguousarray(a) for k, a in arrays.items()}
    nc = bacc.Bacc("TRN2", target_bir_lowering=False, num_devices=1)
    args = [nc.dram_tensor(k, a.shape, mybir.dt.from_np(a.dtype), kind="ExternalInput").ap() for k, a in arrays.items()]
    out = nc.dram_tensor("out_dram", (SEQ, D), F32, kind="ExternalOutput").ap()
    meta_ssd_mla_moe(nc, *args, out)
    r = run_bass_kernel_spmd(nc, [arrays], core_ids=[0])
    return r.results[0]["out_dram"].reshape(1, SEQ, D)
```
